# Optimizing a Trainium2 kernel written in Bass

```python
import math
import jax, jax.numpy as jnp
from jax import lax
import numpy as np

D_MODEL = 1024
BATCH = 1
SEQ = 512
DEPTH = 2

D_FF = 2816
MLSTM_HEADS = 4
MLSTM_HEAD_DIM = 64
MLSTM_WIDTH = MLSTM_HEADS * MLSTM_HEAD_DIM
MLSTM_CHUNK = 64
SSM_HEADS = 8
SSM_HEAD_DIM = 64
SSM_WIDTH = SSM_HEADS * SSM_HEAD_DIM
SSM_STATE = 128
SSM_GROUPS = 2
SSM_CONV = 4
SSM_CONV_DIM = SSM_WIDTH + 2 * SSM_GROUPS * SSM_STATE
SSM_CHUNK = 128
DIFF_HEADS = 4
DIFF_QK_DIM = 32
DIFF_V_DIM = 64
DIFF_WIDTH = DIFF_HEADS * DIFF_V_DIM
Q_BLOCK = 128
REL_BUCKETS = 32
REL_MAX_DIST = 128
D_MIX = MLSTM_WIDTH + SSM_WIDTH + DIFF_WIDTH
IN_SPLIT_SIZES = (MLSTM_WIDTH, MLSTM_WIDTH, MLSTM_WIDTH, MLSTM_WIDTH, MLSTM_HEADS, MLSTM_HEADS,
                  SSM_WIDTH, SSM_CONV_DIM, SSM_HEADS,
                  2 * DIFF_HEADS * DIFF_QK_DIM, 2 * DIFF_HEADS * DIFF_QK_DIM, DIFF_WIDTH)
D_IN = sum(IN_SPLIT_SIZES)
NORM_EPS = 1e-6


def rms_norm(x, w):
    xf = x.astype(jnp.float32)
    y = xf * lax.rsqrt(jnp.mean(xf * xf, axis=-1, keepdims=True) + NORM_EPS)
    return (y * w.astype(jnp.float32)).astype(x.dtype)

def swiglu_ffn(x, w_gate, w_up, w_down):
    return (jax.nn.silu(x @ w_gate) * (x @ w_up)) @ w_down

def t5_bucket(rel):
    n = jnp.maximum(rel, 0)
    max_exact = REL_BUCKETS // 2
    nf = jnp.maximum(n, 1).astype(jnp.float32)
    large = max_exact + (jnp.log(nf / max_exact) / math.log(REL_MAX_DIST / max_exact)
                         * (REL_BUCKETS - max_exact)).astype(jnp.int32)
    large = jnp.minimum(large, REL_BUCKETS - 1)
    return jnp.where(n < max_exact, n, large)

def causal_dwconv(x, w, b):
    K, C = w.shape
    y = lax.conv_general_dilated(x, w[:, None, :], window_strides=(1,), padding=((K - 1, 0),),
                                 dimension_numbers=('NWC', 'WIO', 'NWC'), feature_group_count=C)
    return y + b

def mlstm_chunkwise(q, k, v, i_pre, log_f):
    Bsz, H, S, DK = q.shape
    DV = v.shape[-1]
    L = MLSTM_CHUNK
    nc = S // L

    def to_chunks(a):
        return jnp.moveaxis(a.reshape(a.shape[:2] + (nc, L) + a.shape[3:]), 2, 0)

    causal = jnp.tril(jnp.ones((L, L), dtype=bool))

    def step(carry, inp):
        C, n, m = carry
        qc, kc, vc, ic, fc = inp
        b = jnp.cumsum(fc, axis=-1)
        log_d = jnp.where(causal, b[..., :, None] - b[..., None, :] + ic[..., None, :], -jnp.inf)
        m_inter = b + m[..., None]
        m_t = jnp.maximum(m_inter, jnp.max(log_d, axis=-1))
        d = jnp.exp(log_d - m_t[..., None])
        inter = jnp.exp(m_inter - m_t)
        s = jnp.einsum('bhtd,bhsd->bhts', qc, kc) * d
        num = jnp.einsum('bhts,bhsv->bhtv', s, vc) + inter[..., None] * jnp.einsum('bhtd,bhdv->bhtv', qc, C)
        den = jnp.sum(s, axis=-1) + inter * jnp.einsum('bhtd,bhd->bht', qc, n)
        h = num / jnp.maximum(jnp.abs(den), jnp.exp(-m_t))[..., None]
        b_last = b[..., -1]
        log_w = b_last[..., None] - b + ic
        m_new = jnp.maximum(b_last + m, jnp.max(log_w, axis=-1))
        w = jnp.exp(log_w - m_new[..., None])
        decay = jnp.exp(b_last + m - m_new)
        C_new = decay[..., None, None] * C + jnp.einsum('bhs,bhsd,bhsv->bhdv', w, kc, vc)
        n_new = decay[..., None] * n + jnp.einsum('bhs,bhsd->bhd', w, kc)
        return (C_new, n_new, m_new), h

    init = (jnp.zeros((Bsz, H, DK, DV), jnp.float32), jnp.zeros((Bsz, H, DK), jnp.float32),
            jnp.zeros((Bsz, H), jnp.float32))
    xs = (to_chunks(q), to_chunks(k), to_chunks(v), to_chunks(i_pre), to_chunks(log_f))
    _, h = lax.scan(step, init, xs)
    return jnp.moveaxis(h, 0, 2).reshape(Bsz, H, S, DV)

def ssd_chunked(x, dt, A, Bm, Cm):
    Bsz, S, H, P = x.shape
    N = Bm.shape[-1]
    L = SSM_CHUNK
    nc = S // L
    xc = (x * dt[..., None]).reshape(Bsz, nc, L, H, P)
    Bc = Bm.reshape(Bsz, nc, L, H, N)
    Cc = Cm.reshape(Bsz, nc, L, H, N)
    a_cs = jnp.cumsum((dt * A).reshape(Bsz, nc, L, H).transpose(0, 3, 1, 2), axis=-1)
    causal = jnp.tril(jnp.ones((L, L), dtype=bool))
    seg = jnp.exp(jnp.where(causal, a_cs[..., :, None] - a_cs[..., None, :], -jnp.inf))
    scores = jnp.einsum('bclhn,bcshn->bhcls', Cc, Bc) * seg
    y_diag = jnp.einsum('bhcls,bcshp->bclhp', scores, xc)
    decay_in = jnp.exp(a_cs[..., -1:] - a_cs)
    states = jnp.einsum('bcshn,bhcs,bcshp->bchpn', Bc, decay_in, xc)
    chunk_decay = jnp.exp(a_cs[..., -1])

    def step(s, inp):
        st, dec = inp
        return dec[..., None, None] * s + st, s

    _, prev = lax.scan(step, jnp.zeros((Bsz, H, P, N), jnp.float32),
                       (jnp.moveaxis(states, 1, 0), jnp.moveaxis(chunk_decay, 2, 0)))
    prev = jnp.moveaxis(prev, 0, 1)
    y_off = jnp.einsum('bclhn,bchpn,bhcl->bclhp', Cc, prev, jnp.exp(a_cs))
    return (y_diag + y_off).reshape(Bsz, S, H, P)

def diff_attention(q, k, v, rel_bias, lam):
    Bsz, H, S = q.shape[:3]
    DV = v.shape[-1]
    nb = S // Q_BLOCK
    scale = DIFF_QK_DIM ** -0.5
    k1 = k[..., 0, :]
    k2 = k[..., 1, :]
    qb = jnp.moveaxis(q.reshape(Bsz, H, nb, Q_BLOCK, 2, DIFF_QK_DIM), 2, 0)
    k_pos = jnp.arange(S)

    def block(args):
        qblk, bi = args
        q_pos = bi * Q_BLOCK + jnp.arange(Q_BLOCK)
        rel = q_pos[:, None] - k_pos[None, :]
        mask = rel >= 0
        bias = jnp.moveaxis(rel_bias[t5_bucket(rel)], -1, 0).astype(jnp.float32)

        def probs(qi, ki):
            logits = jnp.einsum('bhqd,bhkd->bhqk', qi, ki).astype(jnp.float32) * scale + bias
            return jax.nn.softmax(jnp.where(mask, logits, -jnp.inf), axis=-1)

        a = probs(qblk[..., 0, :], k1) - lam * probs(qblk[..., 1, :], k2)
        return jnp.einsum('bhqk,bhkv->bhqv', a.astype(v.dtype), v)

    out = lax.map(block, (qb, jnp.arange(nb)))
    return jnp.moveaxis(out, 0, 2).reshape(Bsz, H, S, DV)

def hybrid_mixer(h, layer_idx, w_in, w_out, mlstm_gate_bias, mlstm_norm_w, conv_w, conv_b,
                 dt_bias, A_log, D_skip, ssm_norm_w, q_norm_w, k_norm_w, lambdas, subln_w, rel_bias):
    Bsz, S, _ = h.shape
    f32 = jnp.float32
    proj = h @ w_in
    split_idx = np.cumsum(IN_SPLIT_SIZES)[:-1].tolist()
    mq, mk, mv, mo, mi, mf, z, xbc, dt_raw, dq, dk, dv = jnp.split(proj, split_idx, axis=-1)

    def heads(a, nh):
        return a.reshape(Bsz, S, nh, -1).transpose(0, 2, 1, 3)

    i_pre = (mi + mlstm_gate_bias[0]).astype(f32).transpose(0, 2, 1)
    log_f = jax.nn.log_sigmoid((mf + mlstm_gate_bias[1]).astype(f32)).transpose(0, 2, 1)
    hm = mlstm_chunkwise(heads(mq, MLSTM_HEADS).astype(f32),
                         heads(mk, MLSTM_HEADS).astype(f32) * (MLSTM_HEAD_DIM ** -0.5),
                         heads(mv, MLSTM_HEADS).astype(f32), i_pre, log_f)
    hm = rms_norm(hm.transpose(0, 2, 1, 3), mlstm_norm_w.reshape(MLSTM_HEADS, MLSTM_HEAD_DIM))
    y_mlstm = jax.nn.sigmoid(mo) * hm.reshape(Bsz, S, MLSTM_WIDTH).astype(h.dtype)

    xbc = jax.nn.silu(causal_dwconv(xbc, conv_w, conv_b))
    xs, Bm, Cm = jnp.split(xbc, [SSM_WIDTH, SSM_WIDTH + SSM_GROUPS * SSM_STATE], axis=-1)
    xs = xs.reshape(Bsz, S, SSM_HEADS, SSM_HEAD_DIM).astype(f32)
    rep = SSM_HEADS // SSM_GROUPS
    Bm = jnp.repeat(Bm.reshape(Bsz, S, SSM_GROUPS, SSM_STATE), rep, axis=2).astype(f32)
    Cm = jnp.repeat(Cm.reshape(Bsz, S, SSM_GROUPS, SSM_STATE), rep, axis=2).astype(f32)
    dt = jax.nn.softplus((dt_raw + dt_bias).astype(f32))
    A = -jnp.exp(A_log.astype(f32))
    y = ssd_chunked(xs, dt, A, Bm, Cm) + D_skip.astype(f32)[:, None] * xs
    y = y.reshape(Bsz, S, SSM_WIDTH).astype(h.dtype) * jax.nn.silu(z)
    y_ssm = rms_norm(y.reshape(Bsz, S, SSM_GROUPS, -1),
                     ssm_norm_w.reshape(SSM_GROUPS, -1)).reshape(Bsz, S, SSM_WIDTH)

    dq = rms_norm(dq.reshape(Bsz, S, DIFF_HEADS, 2, DIFF_QK_DIM), q_norm_w).transpose(0, 2, 1, 3, 4)
    dk = rms_norm(dk.reshape(Bsz, S, DIFF_HEADS, 2, DIFF_QK_DIM), k_norm_w).transpose(0, 2, 1, 3, 4)
    dv = heads(dv, DIFF_HEADS)
    lam_init = 0.8 - 0.6 * math.exp(-0.3 * layer_idx)
    lf = lambdas.astype(f32)
    lam = jnp.exp(jnp.sum(lf[0] * lf[1])) - jnp.exp(jnp.sum(lf[2] * lf[3])) + lam_init
    o = diff_attention(dq, dk, dv, rel_bias, lam)
    o = rms_norm(o.transpose(0, 2, 1, 3), subln_w) * (1.0 - lam_init)
    y_diff = o.reshape(Bsz, S, DIFF_WIDTH)

    return jnp.concatenate([y_mlstm, y_ssm, y_diff], axis=-1) @ w_out

def first_inputs(seed: int = 0) -> dict:
    key = jax.random.key(seed)
    ks = jax.random.split(key, 32)
    L = DEPTH
    f32 = jnp.float32

    def nrm(i, shape, scale):
        return scale * jax.random.normal(ks[i], shape, f32)

    def gain(i, shape):
        return 1.0 + 0.1 * jax.random.normal(ks[i], shape, f32)

    x = jax.random.normal(ks[0], (BATCH, SEQ, D_MODEL), f32)
    ffn1_norm_w = gain(1, (L, D_MODEL))
    ffn1_w_gate = nrm(2, (L, D_MODEL, D_FF), D_MODEL ** -0.5)
    ffn1_w_up = nrm(3, (L, D_MODEL, D_FF), D_MODEL ** -0.5)
    ffn1_w_down = nrm(4, (L, D_FF, D_MODEL), D_FF ** -0.5)
    mix_norm_w = gain(5, (L, D_MODEL))
    w_in = nrm(6, (L, D_MODEL, D_IN), D_MODEL ** -0.5)
    mlstm_gate_bias = jnp.stack([nrm(7, (L, MLSTM_HEADS), 0.1),
                                 jnp.linspace(3.0, 6.0, MLSTM_HEADS)[None, :] + nrm(8, (L, MLSTM_HEADS), 0.1)],
                                axis=1)
    mlstm_norm_w = gain(9, (L, MLSTM_WIDTH))
    ssm_conv_w = nrm(10, (L, SSM_CONV, SSM_CONV_DIM), SSM_CONV ** -0.5)
    ssm_conv_b = nrm(11, (L, SSM_CONV_DIM), 0.01)
    dt0 = jnp.exp(jax.random.uniform(ks[12], (L, SSM_HEADS), f32, math.log(1e-3), math.log(1e-1)))
    ssm_dt_bias = dt0 + jnp.log(-jnp.expm1(-dt0))
    ssm_A_log = jnp.log(jax.random.uniform(ks[13], (L, SSM_HEADS), f32, 1.0, 16.0))
    ssm_D = gain(14, (L, SSM_HEADS))
    ssm_norm_w = gain(15, (L, SSM_WIDTH))
    diff_q_norm_w = gain(16, (L, 2, DIFF_QK_DIM))
    diff_k_norm_w = gain(17, (L, 2, DIFF_QK_DIM))
    diff_lambda = nrm(18, (L, 4, DIFF_QK_DIM), 0.1)
    diff_subln_w = gain(19, (L, DIFF_V_DIM))
    rel_bias = nrm(20, (REL_BUCKETS, DIFF_HEADS), 0.5)
    w_out = nrm(21, (L, D_MIX, D_MODEL), D_MIX ** -0.5)
    ffn2_norm_w = gain(22, (L, D_MODEL))
    ffn2_w_gate = nrm(23, (L, D_MODEL, D_FF), D_MODEL ** -0.5)
    ffn2_w_up = nrm(24, (L, D_MODEL, D_FF), D_MODEL ** -0.5)
    ffn2_w_down = nrm(25, (L, D_FF, D_MODEL), D_FF ** -0.5)
    return {'x': x, 'ffn1_norm_w': ffn1_norm_w, 'ffn1_w_gate': ffn1_w_gate, 'ffn1_w_up': ffn1_w_up,
            'ffn1_w_down': ffn1_w_down, 'mix_norm_w': mix_norm_w, 'w_in': w_in,
            'mlstm_gate_bias': mlstm_gate_bias, 'mlstm_norm_w': mlstm_norm_w,
            'ssm_conv_w': ssm_conv_w, 'ssm_conv_b': ssm_conv_b, 'ssm_dt_bias': ssm_dt_bias,
            'ssm_A_log': ssm_A_log, 'ssm_D': ssm_D, 'ssm_norm_w': ssm_norm_w,
            'diff_q_norm_w': diff_q_norm_w, 'diff_k_norm_w': diff_k_norm_w, 'diff_lambda': diff_lambda,
            'diff_subln_w': diff_subln_w, 'rel_bias': rel_bias, 'w_out': w_out,
            'ffn2_norm_w': ffn2_norm_w, 'ffn2_w_gate': ffn2_w_gate, 'ffn2_w_up': ffn2_w_up,
            'ffn2_w_down': ffn2_w_down}

def first_block(x, ffn1_norm_w, ffn1_w_gate, ffn1_w_up, ffn1_w_down, mix_norm_w, w_in,
              mlstm_gate_bias, mlstm_norm_w, ssm_conv_w, ssm_conv_b, ssm_dt_bias, ssm_A_log, ssm_D,
              ssm_norm_w, diff_q_norm_w, diff_k_norm_w, diff_lambda, diff_subln_w, rel_bias, w_out,
              ffn2_norm_w, ffn2_w_gate, ffn2_w_up, ffn2_w_down):
    for l in range(DEPTH):
        x = x + 0.5 * swiglu_ffn(rms_norm(x, ffn1_norm_w[l]), ffn1_w_gate[l], ffn1_w_up[l], ffn1_w_down[l])
        x = x + hybrid_mixer(rms_norm(x, mix_norm_w[l]), l, w_in[l], w_out[l],
                             mlstm_gate_bias[l], mlstm_norm_w[l], ssm_conv_w[l], ssm_conv_b[l],
                             ssm_dt_bias[l], ssm_A_log[l], ssm_D[l], ssm_norm_w[l],
                             diff_q_norm_w[l], diff_k_norm_w[l], diff_lambda[l], diff_subln_w[l],
                             rel_bias)
        x = x + 0.5 * swiglu_ffn(rms_norm(x, ffn2_norm_w[l]), ffn2_w_gate[l], ffn2_w_up[l], ffn2_w_down[l])
    return x


DEPTH_2 = 1

GRID_W = 64
CTX_LEN = 256
MIX_WIDTH = D_MODEL
DN_WIDTH = MIX_WIDTH // 2
DN_HEADS = 4
DN_HEAD_DIM = DN_WIDTH // DN_HEADS
N_DIR = 2
CONV_K = 4
CHUNK = 64
POOL_WIDTH = MIX_WIDTH - DN_WIDTH
POOL_WINDOWS = (2, 4, 8, 16)
POOL_GROUPS = len(POOL_WINDOWS)
POOL_GROUP_DIM = POOL_WIDTH // POOL_GROUPS
N_EXPERTS = 16
EC_CAPACITY = 2
EXPERT_FF = D_MODEL
EPS = 1e-6
QKV_COLS = 3 * DN_WIDTH
GATE_COLS = N_DIR * DN_HEADS
STATE_COLS = QKV_COLS + 2 * GATE_COLS
IN_COLS = STATE_COLS + DN_WIDTH + POOL_WIDTH


def rmsnorm(x, g):
    xf = x.astype(jnp.float32)
    y = xf * lax.rsqrt(jnp.mean(xf * xf, axis=-1, keepdims=True) + EPS)
    return (y * g.astype(jnp.float32)).astype(x.dtype)

def l2norm(x):
    xf = x.astype(jnp.float32)
    return xf * lax.rsqrt(jnp.sum(xf * xf, axis=-1, keepdims=True) + EPS)

def adaln_params(cond, w_mod, b_mod):
    return jnp.split(jax.nn.silu(cond) @ w_mod + b_mod, 6, axis=-1)

def modulate(h, shift, scale):
    return h * (1 + scale) + shift

def window_bounds(n, w):
    pos = jnp.arange(n)
    return jnp.clip(pos - w // 2, 0, n), jnp.clip(pos - w // 2 + w, 0, n)

def centred_box_mean(u, rows):
    B_, L, C = u.shape
    uf = u.astype(jnp.float32)
    outs = []
    if rows is None:
        s = jnp.pad(jnp.cumsum(uf, axis=1), ((0, 0), (1, 0), (0, 0)))
        for i, w in enumerate(POOL_WINDOWS):
            sg = s[..., i * POOL_GROUP_DIM:(i + 1) * POOL_GROUP_DIM]
            lo, hi = window_bounds(L, w)
            cnt = (hi - lo).astype(jnp.float32)
            outs.append((jnp.take(sg, hi, axis=1) - jnp.take(sg, lo, axis=1)) / cnt[None, :, None])
        return jnp.concatenate(outs, axis=-1)
    grid = uf.reshape(B_, rows, GRID_W, C)
    s = jnp.pad(jnp.cumsum(jnp.cumsum(grid, axis=1), axis=2), ((0, 0), (1, 0), (1, 0), (0, 0)))
    for i, w in enumerate(POOL_WINDOWS):
        sg = s[..., i * POOL_GROUP_DIM:(i + 1) * POOL_GROUP_DIM]
        lr, hr = window_bounds(rows, w)
        lc, hc = window_bounds(GRID_W, w)
        s_hi = jnp.take(sg, hr, axis=1)
        s_lo = jnp.take(sg, lr, axis=1)
        tot = (jnp.take(s_hi, hc, axis=2) - jnp.take(s_hi, lc, axis=2)
               - jnp.take(s_lo, hc, axis=2) + jnp.take(s_lo, lc, axis=2))
        cnt = ((hr - lr)[:, None] * (hc - lc)[None, :]).astype(jnp.float32)
        outs.append(tot / cnt[None, :, :, None])
    return jnp.concatenate(outs, axis=-1).reshape(B_, L, C)

def pool_mixer(u, pool_w, pool_scale, rows):
    B_, L, _ = u.shape
    m = (centred_box_mean(u, rows) - u.astype(jnp.float32)).astype(u.dtype)
    m = m.reshape(B_, L, POOL_GROUPS, POOL_GROUP_DIM)
    y = jnp.einsum('blgc,gcd->blgd', m, pool_w).reshape(B_, L, POOL_WIDTH)
    return y * pool_scale

def short_conv(x, w):
    C = x.shape[-1]
    return lax.conv_general_dilated(
        x, w[:, None, :], window_strides=(1,),
        padding=[(CONV_K // 2, CONV_K - 1 - CONV_K // 2)],
        dimension_numbers=('NWC', 'WIO', 'NWC'), feature_group_count=C)

def deltanet_inputs(feat_pre, ab_pre, conv_w, a_log, dt_bias):
    B_, L, _ = feat_pre.shape
    feats = jax.nn.silu(short_conv(feat_pre, conv_w))
    heads = lambda t: jnp.transpose(t.reshape(B_, L, DN_HEADS, DN_HEAD_DIM), (0, 2, 1, 3))
    parts = [heads(t) for t in jnp.split(feats, feats.shape[-1] // DN_WIDTH, axis=-1)]
    ab = ab_pre.astype(jnp.float32).reshape(B_, L, 2, N_DIR, DN_HEADS)
    log_a = -jnp.exp(a_log.astype(jnp.float32)) * jax.nn.softplus(ab[:, :, 0] + dt_bias.astype(jnp.float32))
    beta = jax.nn.sigmoid(ab[:, :, 1])
    to_dir = lambda t: jnp.transpose(t, (2, 0, 3, 1))
    return parts, to_dir(log_a), to_dir(beta)

def chunk_gated_delta(q, k, v, log_a, beta, s0):
    B_, H, L, _ = k.shape
    n = L // CHUNK
    f32 = jnp.float32
    blocks = lambda t: t.astype(f32).reshape(B_, H, n, CHUNK, t.shape[-1])
    kc, vc = blocks(k), blocks(v)
    g = jnp.cumsum(log_a.astype(f32).reshape(B_, H, n, CHUNK), axis=-1)
    bc = beta.astype(f32).reshape(B_, H, n, CHUNK, 1)
    idx = jnp.arange(CHUNK)
    incl = idx[:, None] >= idx[None, :]
    decay = jnp.where(incl, jnp.exp(jnp.minimum(g[..., :, None] - g[..., None, :], 0.0)), 0.0)
    k_beta = kc * bc
    m = jnp.where(idx[:, None] > idx[None, :], jnp.einsum('bhnik,bhnjk->bhnij', k_beta, kc) * decay, 0.0)
    eye = jnp.eye(CHUNK, dtype=f32)
    p = -m
    t_inv = eye + p
    for _ in range(CHUNK.bit_length() - 2):
        p = p @ p
        t_inv = t_inv @ (eye + p)
    w_blk = jnp.einsum('bhnij,bhnjk->bhnik', t_inv, k_beta * jnp.exp(g)[..., None])
    u_blk = jnp.einsum('bhnij,bhnjv->bhniv', t_inv, vc * bc)
    g_last = g[..., -1:]
    k_tail = kc * jnp.exp(g_last - g)[..., None]
    s_decay = jnp.exp(g_last)[..., None]
    first = lambda t: jnp.moveaxis(t, 2, 0)

    def advance(s, w_n, u_n, kt_n, sd_n):
        u_new = u_n - jnp.einsum('bhik,bhkv->bhiv', w_n, s)
        return s * sd_n + jnp.einsum('bhik,bhiv->bhkv', kt_n, u_new), u_new

    if q is None:
        def state_step(s, xs):
            s_next, _ = advance(s, *xs)
            return s_next, None
        s_fin, _ = lax.scan(state_step, s0, tuple(map(first, (w_blk, u_blk, k_tail, s_decay))))
        return None, s_fin

    qc = blocks(q)
    q_dec = qc * jnp.exp(g)[..., None]
    qk = jnp.einsum('bhnik,bhnjk->bhnij', qc, kc) * decay

    def out_step(s, xs):
        w_n, u_n, kt_n, sd_n, qd_n, qk_n = xs
        s_next, u_new = advance(s, w_n, u_n, kt_n, sd_n)
        o_n = jnp.einsum('bhik,bhkv->bhiv', qd_n, s) + jnp.einsum('bhij,bhjv->bhiv', qk_n, u_new)
        return s_next, o_n

    s_fin, o = lax.scan(out_step, s0, tuple(map(first, (w_blk, u_blk, k_tail, s_decay, q_dec, qk))))
    return jnp.moveaxis(o, 0, 2).reshape(B_, H, L, -1), s_fin

def bidir_delta(q, k, v, log_a, beta, s0):
    rev = lambda t: None if t is None else jnp.flip(t, axis=2)
    o_f, s_f = chunk_gated_delta(q, k, v, log_a[0], beta[0], s0[0])
    o_b, s_b = chunk_gated_delta(rev(q), rev(k), rev(v), rev(log_a[1]), rev(beta[1]), s0[1])
    o = None if q is None else o_f + rev(o_b)
    return o, (s_f, s_b)

def token_mixer(h, w_in, conv_w, a_log, dt_bias, dn_norm, pool_w, pool_scale, w_out, s0, rows):
    B_, L, _ = h.shape
    proj = h @ w_in
    (q, k, v), log_a, beta = deltanet_inputs(proj[..., :QKV_COLS], proj[..., QKV_COLS:STATE_COLS],
                                             conv_w, a_log, dt_bias)
    q = l2norm(q) * DN_HEAD_DIM ** -0.5
    k = l2norm(k)
    o, states = bidir_delta(q, k, v, log_a, beta, s0)
    o = jnp.transpose(o, (0, 2, 1, 3))
    gate = proj[..., STATE_COLS:STATE_COLS + DN_WIDTH].reshape(B_, L, DN_HEADS, DN_HEAD_DIM)
    o = (rmsnorm(o, dn_norm) * jax.nn.silu(gate.astype(jnp.float32))).astype(h.dtype)
    o = o.reshape(B_, L, DN_WIDTH)
    pooled = pool_mixer(proj[..., STATE_COLS + DN_WIDTH:], pool_w, pool_scale, rows)
    return jnp.concatenate([o, pooled], axis=-1) @ w_out, states

def context_states(h, w_in, conv_w, a_log, dt_bias, s0):
    proj = h @ w_in[:, DN_WIDTH:STATE_COLS]
    (k, v), log_a, beta = deltanet_inputs(proj[..., :2 * DN_WIDTH], proj[..., 2 * DN_WIDTH:],
                                          conv_w[:, DN_WIDTH:], a_log, dt_bias)
    _, states = bidir_delta(None, l2norm(k), v, log_a, beta, s0)
    return states

def expert_choice_ffn(h, w_router, w_gate, w_up, w_down):
    B_, L, D = h.shape
    cap = EC_CAPACITY * L // N_EXPERTS
    aff = jax.nn.softmax((h @ w_router).astype(jnp.float32), axis=-1)
    top_aff, top_idx = lax.top_k(jnp.swapaxes(aff, 1, 2), cap)
    xe = jax.vmap(lambda hb, ib: hb[ib])(h, top_idx)
    hid = jax.nn.silu(jnp.einsum('becd,edf->becf', xe, w_gate)) * jnp.einsum('becd,edf->becf', xe, w_up)
    ye = jnp.einsum('becf,efd->becd', hid, w_down) * top_aff[..., None].astype(h.dtype)
    combine = lambda ib, yb: jnp.zeros((L, D), yb.dtype).at[ib.reshape(-1)].add(yb.reshape(-1, D))
    return jax.vmap(combine)(top_idx, ye)

def second_inputs(seed: int = 0) -> dict:
    key = jax.random.key(seed)
    ks = jax.random.split(key, 21)
    nrm = lambda k, shape, scale: jax.random.normal(k, shape, jnp.float32) * scale
    D = D_MODEL
    dt = jnp.exp(jax.random.uniform(ks[11], (DEPTH_2, N_DIR, DN_HEADS), jnp.float32,
                                    minval=math.log(1e-3), maxval=math.log(1e-1)))
    return {
        'x': nrm(ks[0], (BATCH, SEQ, D), 1.0),
        'c': nrm(ks[1], (BATCH, D), 1.0),
        'ctx': nrm(ks[2], (BATCH, CTX_LEN, D), 1.0),
        'c_ctx': nrm(ks[3], (D,), 1.0),
        'w_mod': nrm(ks[4], (DEPTH_2, D, 6 * D), 0.5 * D ** -0.5),
        'b_mod': nrm(ks[5], (DEPTH_2, 6 * D), 0.01),
        'norm1': 1.0 + nrm(ks[6], (DEPTH_2, D), 0.02),
        'norm2': 1.0 + nrm(ks[7], (DEPTH_2, D), 0.02),
        'w_in': nrm(ks[8], (DEPTH_2, D, IN_COLS), D ** -0.5),
        'conv_w': nrm(ks[9], (DEPTH_2, CONV_K, QKV_COLS), CONV_K ** -0.5),
        'a_log': jnp.log(jax.random.uniform(ks[10], (DEPTH_2, N_DIR, DN_HEADS), jnp.float32, minval=1.0, maxval=16.0)),
        'dt_bias': dt + jnp.log(-jnp.expm1(-dt)),
        'dn_norm': 1.0 + nrm(ks[12], (DEPTH_2, DN_HEAD_DIM), 0.02),
        'pool_w': nrm(ks[13], (DEPTH_2, POOL_GROUPS, POOL_GROUP_DIM, POOL_GROUP_DIM), POOL_GROUP_DIM ** -0.5),
        'pool_scale': 1.0 + nrm(ks[14], (DEPTH_2, POOL_WIDTH), 0.1),
        'w_out': nrm(ks[15], (DEPTH_2, MIX_WIDTH, D), MIX_WIDTH ** -0.5),
        'w_router': nrm(ks[16], (DEPTH_2, D, N_EXPERTS), D ** -0.5),
        'w_gate': nrm(ks[17], (DEPTH_2, N_EXPERTS, D, EXPERT_FF), D ** -0.5),
        'w_up': nrm(ks[18], (DEPTH_2, N_EXPERTS, D, EXPERT_FF), D ** -0.5),
        'w_down': nrm(ks[19], (DEPTH_2, N_EXPERTS, EXPERT_FF, D), EXPERT_FF ** -0.5),
        'norm_f': 1.0 + nrm(ks[20], (D,), 0.02),
    }

def second_block(x, c, ctx, c_ctx, w_mod, b_mod, norm1, norm2, w_in, conv_w, a_log, dt_bias, dn_norm,
              pool_w, pool_scale, w_out, w_router, w_gate, w_up, w_down, norm_f):
    rows = x.shape[1] // GRID_W
    zero = jnp.zeros((ctx.shape[0], DN_HEADS, DN_HEAD_DIM, DN_HEAD_DIM), jnp.float32)
    z = ctx
    for l in range(DEPTH_2):
        mix_w = (w_in[l], conv_w[l], a_log[l], dt_bias[l], dn_norm[l], pool_w[l], pool_scale[l], w_out[l])
        csh1, csc1, cg1, csh2, csc2, cg2 = adaln_params(c_ctx, w_mod[l], b_mod[l])
        sh1, sc1, g1, sh2, sc2, g2 = [t[:, None, :] for t in adaln_params(c, w_mod[l], b_mod[l])]
        hz = modulate(rmsnorm(z, norm1[l]), csh1, csc1)
        if l < DEPTH_2 - 1:
            yz, ctx_st = token_mixer(hz, *mix_w, (zero, zero), None)
            z = z + cg1 * yz
            hz2 = modulate(rmsnorm(z, norm2[l]), csh2, csc2)
            z = z + cg2 * expert_choice_ffn(hz2, w_router[l], w_gate[l], w_up[l], w_down[l])
        else:
            ctx_st = context_states(hz, w_in[l], conv_w[l], a_log[l], dt_bias[l], (zero, zero))
        h = modulate(rmsnorm(x, norm1[l]), sh1, sc1)
        y, _ = token_mixer(h, *mix_w, ctx_st, rows)
        x = x + g1 * y
        h = modulate(rmsnorm(x, norm2[l]), sh2, sc2)
        x = x + g2 * expert_choice_ffn(h, w_router[l], w_gate[l], w_up[l], w_down[l])
    return rmsnorm(x, norm_f)


def setup_inputs(seed=0):
    out = dict(first_inputs(seed))
    for name, value in second_inputs(seed + 1).items():
        if name != "x":
            out[name + "_2"] = value
    return out


def reference(
    x, ffn1_norm_w, ffn1_w_gate, ffn1_w_up, ffn1_w_down, mix_norm_w, w_in, mlstm_gate_bias,
    mlstm_norm_w, ssm_conv_w, ssm_conv_b, ssm_dt_bias, ssm_A_log, ssm_D, ssm_norm_w,
    diff_q_norm_w, diff_k_norm_w, diff_lambda, diff_subln_w, rel_bias, w_out, ffn2_norm_w,
    ffn2_w_gate, ffn2_w_up, ffn2_w_down, c_2, ctx_2, c_ctx_2, w_mod_2, b_mod_2, norm1_2,
    norm2_2, w_in_2, conv_w_2, a_log_2, dt_bias_2, dn_norm_2, pool_w_2, pool_scale_2, w_out_2,
    w_router_2, w_gate_2, w_up_2, w_down_2, norm_f_2,
):
    x = first_block(
        x, ffn1_norm_w, ffn1_w_gate, ffn1_w_up, ffn1_w_down, mix_norm_w, w_in, mlstm_gate_bias,
        mlstm_norm_w, ssm_conv_w, ssm_conv_b, ssm_dt_bias, ssm_A_log, ssm_D, ssm_norm_w,
        diff_q_norm_w, diff_k_norm_w, diff_lambda, diff_subln_w, rel_bias, w_out, ffn2_norm_w,
        ffn2_w_gate, ffn2_w_up, ffn2_w_down,
    )
    return second_block(
        x, c_2, ctx_2, c_ctx_2, w_mod_2, b_mod_2, norm1_2, norm2_2, w_in_2, conv_w_2, a_log_2,
        dt_bias_2, dn_norm_2, pool_w_2, pool_scale_2, w_out_2, w_router_2, w_gate_2, w_up_2,
        w_down_2, norm_f_2,
    )


_drawn_inputs = setup_inputs


def setup_inputs(seed=0):
    import zlib

    import numpy as np

    out = dict(_drawn_inputs(seed))
    spreads = {}
    factors = {'ssm_conv_b': 5.277,
     'ctx_2': 6.973,
     'c_ctx_2': 8.0,
     'b_mod_2': 8.0,
     'norm1_2': 8.0,
     'norm2_2': 8.0,
     'a_log_2': 3.73,
     'dn_norm_2': 8.0,
     'pool_scale_2': 4.297,
     'norm_f_2': 2.827}
    for name, (base, spread) in spreads.items():
        noise = np.random.default_rng([zlib.crc32(name.encode()), seed]).standard_normal(out[name].shape)
        drawn = base * np.exp(spread * noise) if base else spread * noise
        out[name] = __import__('jax').numpy.asarray(drawn.astype(out[name].dtype))
    for name, factor in factors.items():
        out[name] = (out[name] * factor).astype(out[name].dtype)
    return out
```

```python
import numpy as np

import concourse.bass as bass
import concourse.mybir as mybir
from concourse.alu_op_type import AluOpType as ALU

F32 = mybir.dt.float32
FR = mybir.dt.float32r
U32 = mybir.dt.uint32
ACT = mybir.ActivationFunctionType
AX = mybir.AxisListType.X

T = 512
D = 1024
FF = 2816
NF = FF // 128
BIG = 1.0e30
MEM_AT = 16512
EPS = 1e-6
NSLOT = 4
SLOT = 2048

CONSTS = ["ident", "one", "b32", "GT", "LE", "LT", "GE", "NEGU", "bd"]


def const_arrays():
    p = np.arange(128)[:, None]
    j = np.arange(128)[None, :]
    c = {
        "ident": p == j, "one": np.ones((128, 128)), "b32": (p // 32 == j // 32) / 32.0,
        "GT": p > j, "LE": p <= j, "LT": p < j, "GE": p >= j,
        "NEGU": np.where(p <= j, 0.0, BIG), "bd": p // 64 == j // 64,
    }
    k = np.concatenate([np.asarray(c[n], np.float32) for n in CONSTS], 1)
    sel = np.zeros((4, 4, 128), np.float32)
    for h in range(4):
        sel[h, h] = 1.0
    rel = 511 - np.arange(640)
    n = np.maximum(rel, 0)
    nf = np.maximum(n, 1).astype(np.float32)
    large = 16 + (np.log(nf / np.float32(16)) / np.float32(np.log(8.0)) * np.float32(16)).astype(np.int32)
    bucket = np.where(n < 16, n, np.minimum(large, 31))
    oh = ((bucket[None, :] == np.arange(32)[:, None]) & (rel >= 0)[None, :]).astype(np.float32)
    neg = np.tile(np.where(rel < 0, np.float32(-BIG), np.float32(0.0)), (128, 1))
    box = np.zeros((4, 512, 512), np.float32)
    for g, w in enumerate((2, 4, 8, 16)):
        def bounds(m):
            q = np.arange(m)
            return np.clip(q - w // 2, 0, m), np.clip(q - w // 2 + w, 0, m)
        lr, hr = bounds(8)
        lc, hc = bounds(64)
        R = ((np.arange(8)[None] >= lr[:, None]) & (np.arange(8)[None] < hr[:, None])) * 1.0
        C = ((np.arange(64)[None] >= lc[:, None]) & (np.arange(64)[None] < hc[:, None])) * 1.0
        cnt = ((hr - lr)[:, None] * (hc - lc)[None, :]).astype(np.float64).reshape(512)
        K = np.kron(R, C) / cnt[:, None] - np.eye(512)
        box[g] = K.T
    box = box.reshape(4, 4, 128, 512).transpose(0, 2, 1, 3).reshape(4, 128, 2048)
    return k, sel.reshape(4, 512), oh, neg.astype(np.float32), np.ascontiguousarray(box)


COLS = [(f"{n}{l}", w) for l in range(2) for n, w in
        (("n1_", 8), ("nm_", 8), ("n2_", 8), ("cw_", 32), ("cb_", 8), ("qw_", 1), ("kw_", 1))] + [
    ("norm1", 8), ("norm2", 8), ("normf", 8), ("cw2", 48), ("psc", 4), ("c", 16), ("bmod", 48)]
ROWS = [(f"{n}{l}", w) for l in range(2) for n, w in
        (("gb_", 64), ("al_", 32), ("mn_", 256), ("sn_", 512), ("D_", 8), ("sl_", 64), ("lam_", 128))] + [
    ("al2", 8), ("dtb2", 8), ("dn", 128)]


def offsets(spec):
    out, at = {}, 0
    for n, w in spec:
        out[n] = (at, w)
        at += w
    return out, at


class Eng:

    def __init__(self, nc, h, name):
        self.h, self.q, self.n, self.seen = h, [], 0, {}
        self.sem = nc.alloc_semaphore("s_" + name)
        self.name = name

    def wait(self, *toks):
        for t in toks:
            if t is None:
                continue
            if isinstance(t, list):
                self.wait(*t)
                continue
            sem, v = t
            if self.seen.get(sem.name, 0) < v:
                self.seen[sem.name] = v
                self.q.append(lambda sem=sem, v=v: self.h.wait_ge(sem, v))

    def __call__(self, fn, *toks):
        self.wait(*toks)
        self.n += 1
        self.q.append(lambda: fn(self.h).then_inc(self.sem, 1))
        return (self.sem, self.n)

    def quiet(self, fn, *toks):
        self.wait(*toks)
        self.q.append(lambda: fn(self.h))

    def dma(self, fn, sem, *toks):
        self.wait(*toks)
        self.q.append(lambda: fn(self.h).then_inc(sem, 16))

    def now(self):
        return (self.sem, self.n) if self.n else None

    def run(self):
        for f in self.q:
            f()


class Bank:
    def __init__(self, ap, i, w, owner):
        self.ap, self.i, self.w, self.owner = ap, i, w, owner

    def free(self, *toks):
        self.owner.freed[self.i] = list(toks)
        self.owner.busy[self.i] = False


class Banks:

    def __init__(self, aps):
        self.aps, self.k = aps, -1
        self.freed = [[] for _ in aps]
        self.busy = [False] * len(aps)

    def take(self):
        for _ in self.aps:
            self.k = (self.k + 1) % len(self.aps)
            if not self.busy[self.k]:
                self.busy[self.k] = True
                return Bank(self.aps[self.k], self.k, self.freed[self.k], self)
        raise AssertionError("no bank")


def build(nc, A, out_x, dbg=None, upto=99):
    PE, V, S, G, SP = (Eng(nc, h, n) for h, n in (
        (nc.tensor, "pe"), (nc.vector, "dve"), (nc.scalar, "act"), (nc.gpsimd, "pool"), (nc.sync, "sp")))
    banks = Banks([nc.alloc_psum_tensor(f"ps{i}", [128, 512], F32) for i in range(8)])
    NM = 53000
    memu = nc.alloc_sbuf_tensor_at("memu", [128, 192], U32, offset=MEM_AT + 4 * NM)
    top = [0]

    where = {}

    def at(a, n, dt=F32):
        h = nc.alloc_sbuf_tensor_at(f"b{len(where)}", [128, n], dt, offset=MEM_AT + 4 * a)
        where[h.name] = a
        return h[:, :]

    def al(n):
        a = top[0]
        top[0] += (n + 7) // 8 * 8
        assert top[0] <= NM, (top[0], NM)
        return at(a, n)

    def fr(ap):
        return at(where[ap.tensor.name] + ap.offset, ap.shape[1], FR)

    def v3(ap, a):
        return ap.rearrange("p (a b) -> p a b", a=a)

    def v4(ap, a, b):
        return ap.rearrange("p (a b c) -> p a b c", a=a, b=b)

    ring = [al(SLOT) for _ in range(NSLOT)]
    ring_sem = [nc.alloc_semaphore(f"ring{i}") for i in range(NSLOT)]
    ring_n = [0] * NSLOT
    ring_free = [None] * NSLOT
    ring_k = [0]

    class Slot:
        pass

    def load(src, n=SLOT):
        i = ring_k[0] % NSLOT
        ring_k[0] += 1
        assert ring_free[i] != "busy", "slot"
        SP.dma(lambda h: h.dma_start(ring[i][:, 0:n], src), ring_sem[i], ring_free[i])
        ring_n[i] += 1
        ring_free[i] = "busy"
        s = Slot()
        s.ap, s.t, s.i = ring[i][:, 0:n], (ring_sem[i], 16 * ring_n[i]), i
        return s

    def done(s, *toks):
        ring_free[s.i] = list(toks)

    nsem = [0]
    dma_all = []

    def misc(E, dst, src, *toks, slow=False):
        sem = nc.alloc_semaphore(f"m{nsem[0]}")
        nsem[0] += 1
        E.dma(lambda h: h.dma_start(dst, src, allow_slow_non_contiguous=slow), sem, *toks)
        dma_all.append((sem, 16))
        return (sem, 16)

    def snap(name, ap, *toks):
        if dbg is not None:
            t = nc.dram_tensor("dbg_" + name, list(ap.shape), ap.dtype, kind="ExternalOutput")
            dbg.append("dbg_" + name)
            tk = misc(G, t.ap(), ap, *toks, V.now(), S.now(), PE.now())
            for e in (PE, V, S):
                e.wait(tk)

    def every():
        return [e.now() for e in (PE, V, S, G)] + dma_all[-40:]

    def barrier():
        t = every()
        for e in (PE, V, S, G):
            e.wait(*t)

    def mm(out, l, r, *w, start=True, stop=True, inc=False):
        f = lambda h: h.matmul(out, l, r, start=start, stop=stop)
        return PE(f, *w) if inc else PE.quiet(f, *w)

    def tr(out, i, *w, inc=False):
        k = i.shape[0]
        f = lambda h: h.transpose(out, i, ident[0:k, 0:k])
        return PE(f, *w) if inc else PE.quiet(f, *w)

    def tt(out, a, b, op, *w, E=None):
        return (E or V)(lambda h: h.tensor_tensor(out, a, b, op), *w)

    def ts(out, a, s1, op0, *w, s2=None, op1=None, E=None):
        if op1 is None:
            return (E or V)(lambda h: h.tensor_scalar(out, a, s1, None, op0), *w)
        return (E or V)(lambda h: h.tensor_scalar(out, a, s1, s2, op0, op1), *w)

    def stt(out, a, s, b, op0, op1, *w):
        return V(lambda h: h.scalar_tensor_tensor(out, a, s, b, op0, op1), *w)

    def cp(out, a, *w, E=None):
        if E is S:
            return S(lambda h: h.copy(out, a), *w)
        return (E or V)(lambda h: h.tensor_copy(out, a), *w)

    def act(out, a, f, *w, bias=0.0, scale=1.0, acc=None):
        if acc is not None:
            return S(lambda h: h.activation(out, a, f, bias=bias, scale=scale, accum_out=acc), *w)
        return S(lambda h: h.activation(out, a, f, bias=bias, scale=scale), *w)

    def rcp(out, a, *w):
        return V(lambda h: h.reciprocal(out, a), *w)

    class Unit:
        def __init__(self, hi, lo, i, w, owner):
            self.hi, self.lo, self.i, self.w, self.owner = hi, lo, i, w, owner

        def free(self, *t):
            self.owner.freed[self.i] = list(t)

    class Units:

        def __init__(self, region, n):
            self.n, self.k = n, -1
            self.hi = [fr(region[:, 2 * n * i:2 * n * i + n]) for i in range(region.shape[1] // (2 * n))]
            self.lo = [fr(region[:, 2 * n * i + n:2 * n * i + 2 * n]) for i in range(region.shape[1] // (2 * n))]
            self.freed = [[] for _ in self.hi]

        def take(self):
            self.k = (self.k + 1) % len(self.hi)
            return Unit(self.hi[self.k], self.lo[self.k], self.k, self.freed[self.k], self)

    def split(hi, lo, src, *w):
        t1 = cp(hi, src, *w, E=S)
        t2 = tt(lo, src, hi.bitcast(F32), ALU.subtract, t1)
        return [t1, t2]

    def mm3(out, l, r, *w, start, stop, inc):
        mm(out, l[0], r[0], *w, start=start, stop=False)
        mm(out, l[0], r[1], start=False, stop=False)
        return mm(out, l[1], r[0], start=False, stop=stop, inc=inc)

    kst = al(128 * len(CONSTS))
    K = {n: kst[:, i * 128:(i + 1) * 128] for i, n in enumerate(CONSTS)}
    ident = K["ident"]
    sel = al(512)
    coff, cn = offsets(COLS)
    roff, rn = offsets(ROWS)
    cols, rows = al(cn), al(rn)
    smw = al(512)
    poolw = al(512)
    t_c = [misc(S, kst, A["k_const"]), misc(S, sel[0:4, :], A["k_sel"]), misc(S, cols, A["cols"]),
           misc(S, rows, A["rows"]), misc(S, smw, A["smallw"]), misc(S, poolw, A["poolw"])]
    for e in (PE, V, S, G):
        e.wait(*t_c)
    swh, swl = fr(al(512)), fr(al(512))
    tsw = split(swh, swl, smw)
    PE.wait(*tsw)

    def col(n, i=0, w=1):
        return cols[:, coff[n][0] + i:coff[n][0] + i + w]

    def row(n):
        return rows[:, roff[n][0]:roff[n][0] + roff[n][1]]

    xT = v3(al(4096), 8)
    hTf = al(4096)
    hT = v3(hTf, 8)
    rstd = al(512)
    b4f = al(2048)
    bias4 = v3(b4f, 4)
    ctxS = v3(al(1024), 8)
    MOD = v3(al(96), 48)
    A1 = al(8)
    A2 = al(8)
    Ac = al(8)
    hs = al(128 * 4)
    base = top[0]
    print('base', base) if dbg is not None else None
    KD = [True]

    def reset():
        top[0] = base

    two = [al(512), al(512)]
    two_t = [None, None]
    nacc = rstd
    stat = {"acc": None}
    base = top[0]

    def stat_add(k, src, tok):
        n = src.shape[1]
        q = two[k % 2][:, 0:n]
        t = act(nacc[:, 0:n] if k == 0 else q, src, ACT.Square, tok, two_t[k % 2],
                stat["acc"] if k == 0 else None)
        if k:
            t = tt(nacc[:, 0:n], nacc[:, 0:n], q, ALU.add, t, stat["acc"])
            two_t[k % 2] = t
        stat["acc"] = t

    def norm_fm(src, dst, scale_col, n, shift_col=None, full=None):
        b = banks.take()
        p = mm(b.ap[:, 0:n], K["one"], nacc[:, 0:n], stat["acc"], *b.w, inc=True)
        stat["acc"] = p
        r = rstd[:, 0:n]
        t = ts(r, b.ap[:, 0:n], 1.0 / D, ALU.mult, p, s2=EPS, op1=ALU.add)
        b.free(t)
        t = rcp(r, r, t)
        t = act(r, r, ACT.Sqrt, t)
        out = []
        for k in range(8):
            tmp = two[k % 2][:, 0:n] if full is None else full[:, k, :]
            u = stt(tmp, src[:, k, :], scale_col(k), r, ALU.mult, ALU.mult, t, two_t[k % 2])
            if shift_col is not None:
                u = ts(tmp, tmp, shift_col(k), ALU.add, u)
            hi, lo = dst(k)
            out.append(split(hi, lo, tmp, u))
            if full is None:
                two_t[k % 2] = out[-1]
        return out

    def to_fm(src_tok, dst, nt, dep, stats=False):
        last = []
        for k in range(8):
            b = banks.take()
            for t in range(nt):
                p = tr(b.ap[:, t * 128:(t + 1) * 128], src_tok[:, t, k * 128:(k + 1) * 128], dep, *b.w, inc=(t == nt - 1))
            e = cp(dst[:, k, :], b.ap[:, 0:nt * 128], p, E=(S if k % 2 else None))
            b.free(e)
            last.append(e)
            if stats:
                stat_add(k, dst[:, k, :], e)
        return last

    def fm_parts(src, dst, dep):
        b = banks.take()
        for i in range(4):
            p = tr(b.ap[:, i * 128:(i + 1) * 128], src(i), dep, *b.w, inc=(i == 3))
        t = split(dst[0], dst[1], b.ap[:, :], p)
        b.free(*t)
        return t

    def silu(dst, src, tmp, *w):
        t = act(tmp, src, ACT.Tanh, *w, scale=0.5)
        t = ts(tmp, tmp, 0.5, ALU.mult, t, s2=0.5, op1=ALU.add)
        return tt(dst, src, tmp, ALU.mult, t)

    def softplus(dst, x, e, u, d, *w):
        t = act(d, x, ACT.Abs, *w)
        t = act(e, d, ACT.Exp, t, scale=-1.0)
        t = ts(u, e, 1.0, ALU.add, t)
        t2 = act(dst, u, ACT.Ln, t)
        t = ts(d, u, -1.0, ALU.add, t)
        t = tt(e, e, d, ALU.subtract, t)
        t = tt(dst, dst, e, ALU.add, t, t2)
        return stt(dst, x, 0.0, dst, ALU.max, ALU.add, t)

    def rms_tok(Y, G_, W, sq, ms, wrow, extra, *w):
        a = Y.shape[1]
        t = None
        for i in range(a):
            t = tt(sq[:, i], Y[:, i], Y[:, i], ALU.mult, *w)
        t = V(lambda h: h.tensor_reduce(ms, sq, AX, ALU.add), t)
        t = ts(ms, ms, 1.0 / W, ALU.mult, t, s2=EPS, op1=ALU.add)
        t = rcp(ms, ms, t)
        t = act(ms, ms, ACT.Sqrt, t)
        bc = ms.unsqueeze(3).to_broadcast([128, a, G_, W])
        for i in range(a):
            t1 = tt(Y[:, i], Y[:, i], bc[:, i], ALU.mult, t, *w)
            t1 = tt(Y[:, i], Y[:, i], wrow, ALU.mult, t1)
            if extra is not None:
                t1 = ts(Y[:, i], Y[:, i], extra, ALU.mult, t1) if isinstance(extra, float) else \
                    tt(Y[:, i], Y[:, i], extra[:, i], ALU.mult, t1)
        return t1

    def transposes(src, dst, n, w, *dep):
        toks = []
        for j in range(0, n, 4):
            b = banks.take()
            m = min(4, n - j)
            for i in range(m):
                p = tr(b.ap[0:w, i * 128:(i + 1) * 128], src(j + i), *dep, *b.w, inc=(i == m - 1))
            e = cp(dst(j), v3(b.ap[0:w, 0:m * 128], m), p, E=(S if (j // 4) % 2 else None))
            b.free(e)
            toks.append(e)
        return toks

    hlo = [None]

    def parts(hi, lo, n=512):
        h, l = v3(fr(hi), 8), v3(fr(lo), 8)
        return lambda k: (h[:, k, 0:n], l[:, k, 0:n])

    def pipeline(items, ahead):
        for j in range(min(ahead, len(items))):
            items[j][0]()
        for i, (_, mm_, post) in enumerate(items):
            if i + ahead < len(items):
                items[i + ahead][0]()
            mm_()
            post()

    def ffn(idx, nm):
        reset()
        barrier()
        lo = al(4096)
        hp = parts(hTf, lo)
        GRP = (12, 10)
        ahi, alo = v3(fr(al(12 * 512)), 12), v3(fr(al(12 * 512)), 12)
        U = Units(al(8192), 1024)
        sl = {}
        th = []
        ready, st = {}, {"afree": None}
        items = []

        def up_item(f, fi, q):
            x = {}

            def split_():
                if f % 2 == 0:
                    sl[q] = [load(A["wg" if q == 0 else "wu"][idx, f // 2]), []]
                s, rel = sl[q]
                c = slice((f % 2) * 128, (f % 2) * 128 + 128)
                u = x["u"] = U.take()
                x["tw"] = split(v3(u.hi, 8), v3(u.lo, 8), v3(s.ap, 8)[:, :, c], s.t, *u.w)
                rel.append(x["tw"])
                if f % 2:
                    done(s, *rel)

            def mm_():
                u = x["u"]
                b = x["b"] = banks.take()
                for k in range(8):
                    t = mm3(b.ap[:, :], (v3(u.hi, 8)[:, k, :], v3(u.lo, 8)[:, k, :]), hp(k), x["tw"], th[k], *b.w,
                            start=(k == 0), stop=(k == 7), inc=(k == 7))
                u.free(t)
                st[q] = (b, t)

            def post():
                if q == 0:
                    return
                (bg, tg), (bu, tu) = st[0], st[1]
                e = two[f % 2]
                t = act(e, bg.ap[:, :], ACT.Tanh, tg, two_t[f % 2], scale=0.5)
                t = stt(e, e, 1.0, bg.ap[:, :], ALU.add, ALU.mult, t)
                bg.free(t)
                t = tt(e, e, bu.ap[:, :], ALU.mult, t, tu)
                bu.free(t)
                t = split(ahi[:, fi, :], alo[:, fi, :], e, t, st["afree"])
                two_t[f % 2] = t
                ready[fi] = t
            return split_, mm_, post

        def down_item(grp, nf, d, half):
            x = {}
            m = nf // 2

            def split_():
                if half == 0:
                    sl["d"] = [load(A["wd%d" % grp][idx, d], nf * 128), []]
                s, rel = sl["d"]
                u = x["u"] = U.take()
                x["hi"], x["lo"] = (v3(y[:, 0:m * 128], m) for y in (u.hi, u.lo))
                x["tw"] = split(x["hi"], x["lo"], v3(s.ap, nf)[:, half * m:half * m + m, :], s.t, *u.w)
                rel.append(x["tw"])
                if half:
                    done(s, *rel)

            def mm_():
                if half == 0:
                    st["b"] = banks.take()
                b = st["b"]
                for j in range(m):
                    n = half * m + j
                    t = mm3(b.ap[:, :], (x["hi"][:, j, :], x["lo"][:, j, :]), (ahi[:, n, :], alo[:, n, :]), x["tw"],
                            ready[n], *b.w, start=(n == 0), stop=(n == nf - 1), inc=(j == m - 1))
                x["u"].free(t)
                x["t"] = st["afree"] = t

            def post():
                if half == 0:
                    return
                b = st["b"]
                e = stt(xT[:, d, :], b.ap[:, :], 0.25, xT[:, d, :], ALU.mult, ALU.add, x["t"])
                b.free(e)
                if grp == 1:
                    stat_add(d, xT[:, d, :], e)
            return split_, mm_, post

        f0 = 0
        for grp, nf in enumerate(GRP):
            items += [up_item(f0 + fi, fi, q) for fi in range(nf) for q in range(2)]
            items += [down_item(grp, nf, d, half) for d in range(8) for half in range(2)]
            f0 += nf
        for j in range(2):
            items[j][0]()
        items[0] = (lambda: None,) + items[0][1:]
        items[1] = (lambda: None,) + items[1][1:]
        th += norm_fm(xT, hp, lambda k: col(nm, k), 512)
        pipeline(items, 2)

    def fm_items(src, nt, w, put, dep, U):
        sl = {}

        def item(i):
            x = {}

            def split_():
                if i == 0:
                    sl["s"] = [load(w), []]
                s, rel = sl["s"]
                u = x["u"] = U.take()
                x["tw"] = split(v3(u.hi, 8), v3(u.lo, 8), v3(s.ap, 8)[:, :, i * 128:(i + 1) * 128], s.t, *u.w)
                rel.append(x["tw"])
                if i:
                    done(s, *rel)

            def mm_():
                u = x["u"]
                hi, lo = v3(u.hi, 8), v3(u.lo, 8)
                b = x["b"] = banks.take()
                for k in range(8):
                    t = mm3(b.ap[:, 0:nt], (hi[:, k, :], lo[:, k, :]), src(k), x["tw"], dep[k], *b.w,
                            start=(k == 0), stop=(k == 7), inc=(k == 7))
                u.free(t)
                x["t"] = t

            def post():
                x["b"].free(put(i, x["b"].ap[:, 0:nt], x["t"]))
            return split_, mm_, post
        return [item(0), item(1)]

    def tok_items(src, nt, w, put, dep, U):
        sl = {}

        def item(half):
            x = {}

            def split_():
                if half == 0:
                    sl["s"] = [load(w), []]
                s, rel = sl["s"]
                u = x["u"] = U.take()
                x["tw"] = split(v3(u.hi, 4), v3(u.lo, 4), v3(s.ap, 8)[:, 4 * half:4 * half + 4, :], s.t, *u.w)
                rel.append(x["tw"])
                if half:
                    done(s, *rel)

            def mm_():
                if half == 0:
                    sl["b"] = [banks.take() for _ in range(nt)]
                u = x["u"]
                hi, lo = v3(u.hi, 4), v3(u.lo, 4)
                x["t"] = []
                for i in range(nt):
                    c = slice(i * 128, (i + 1) * 128)
                    b = sl["b"][i]
                    for j in range(4):
                        k = 4 * half + j
                        y = src(k)
                        t = mm3(b.ap[:, 0:256], (y[0][:, c], y[1][:, c]), (hi[:, j, :], lo[:, j, :]), x["tw"], dep[k],
                                *b.w, start=(k == 0), stop=(k == 7), inc=(j == 3))
                    x["t"].append(t)
                u.free(t)

            def post():
                if half:
                    for i in range(nt):
                        b = sl["b"][i]
                        b.free(put(i, b.ap[:, 0:256], x["t"][i]))
            return split_, mm_, post
        return [item(0), item(1)]

    def proj_small(src, nt, w, dst, dep):
        hi, lo = (v3(x[:, 128 * w:128 * w + 128], 8) for x in (swh, swl))
        b = banks.take()
        for i in range(nt):
            c = slice(i * 128, (i + 1) * 128)
            for k in range(8):
                x = src(k)
                t = mm3(b.ap[:, 16 * i:16 * i + 16], (x[0][:, c], x[1][:, c]), (hi[:, k, :], lo[:, k, :]), dep[k],
                        *b.w, start=(k == 0), stop=(k == 7), inc=(k == 7))
        e = cp(dst, v3(b.ap[:, 0:16 * nt], nt), t)
        b.free(e)
        return e

    def rel_table():
        reset()
        oh, rb, neg, F = al(640), al(4), al(640), v3(al(2560), 4)
        t = [misc(S, oh[0:32, :], A["k_oh"]), misc(S, rb[0:32, :], A["rel_bias"]), misc(S, neg, A["k_neg"])]
        es = []
        for h in range(4):
            l = rb[0:32, h:h + 1].to_broadcast([32, 128])
            for c0, n in ((0, 512), (512, 128)):
                b = banks.take()
                p = mm(b.ap[:, 0:n], l, oh[0:32, c0:c0 + n], *t, *b.w, inc=True)
                e = tt(F[:, h, c0:c0 + n], b.ap[:, 0:n], neg[:, c0:c0 + n], ALU.add, p, *t)
                b.free(e)
                es.append(e)
        Fd = nc.dram_tensor("F_scratch", [4, 128, 640], F32)
        t = misc(S, Fd.ap().rearrange("h p x -> p h x"), F, *es)
        src = bass.AP(tensor=Fd, offset=127, ap=[[639, 128], [128 * 640, 4], [1, 512]])
        return misc(S, bias4, src, t)

    def mixer(l):
        reset()
        barrier()
        lam_init = 0.8 - 0.6 * float(np.exp(-0.3 * l))
        G1 = v3(al(64), 4)
        SPx, e1, u1, d1, X = (v3(al(48), 4) for _ in range(5))
        Lc = v3(al(48), 4)
        TOT = v3(al(48), 4)
        Bg, cc, mt, em = (v3(al(16), 4) for _ in range(4))
        V1 = al(4 * 4 * 65).rearrange("p (t h c) -> p t h c", t=4, h=4)
        mo = v3(al(1024), 4)
        z = v3(al(2048), 4)
        dvt = v3(al(1024), 4)
        Yf = al(4096)
        Y = v3(Yf, 4)
        small = [al(64) for _ in range(12)]
        qkf = al(4096)
        qk, dqk = v3(qkf[:, 0:2048], 4), v3(qkf[:, 2048:4096], 4)
        xbc = v3(al(8 * 516), 8)
        tAB = al(4096)
        tA, tB, tC = tAB[:, 0:2048], tAB[:, 2048:4096], al(2048)
        crow, Mrow = tA[:, 0:512], tC[:, 1536:2048]
        U = Units(tAB, 1024)
        hp = parts(hTf, Yf)
        th = norm_fm(xT, hp, lambda k: col(f"nm_{l}", k), 512)
        tg = proj_small(hp, 4, l, G1, th)
        win = A["win"]
        items = []
        tq, tv, tz, tdv, tx, td = [], [], [], [], [], []
        for blk in range(2):
            def put(i, ps, t, blk=blk):
                tq.append(cp(qk[:, 2 * blk + i, :], ps, t, E=S))
                return tq[-1]
            items += fm_items(hp, 512, win[l, blk], put, th, U)
        ti_ = V(lambda h: h.memset(V1[:, :, :, 64:65], 1.0))

        def put(i, ps, t):
            tv.append(cp(V1[:, i, :, 0:64], v3(ps, 4), t))
            return tv[-1]
        items += tok_items(hp, 4, win[l, 8], put, th, U)

        def put(i, ps, t):
            tv.append(cp(mo[:, i, :], ps, t, E=S))
            return tv[-1]
        items += tok_items(hp, 4, win[l, 9], put, th, U)
        for half in range(2):
            def put(i, ps, t, half=half):
                tz.append(cp(z[:, i, half * 256:half * 256 + 256], ps, t, E=S))
                return tz[-1]
            items += tok_items(hp, 4, win[l, 10 + half], put, th, U)

        def put(i, ps, t):
            tdv.append(cp(dvt[:, i, :], ps, t, E=S))
            return tdv[-1]
        items += tok_items(hp, 4, win[l, 12], put, th, U)
        tzero = V(lambda h: h.memset(xbc[:, :, 0:3], 0.0))
        for blk in range(4):
            def put(i, ps, t, blk=blk):
                tx.append(cp(xbc[:, 2 * blk + i, 3:515], ps, t, E=(S if i else None)))
                return tx[-1]
            items += fm_items(hp, 512, win[l, 2 + blk], put, th, U)
        for blk in range(2):
            def put(i, ps, t, blk=blk):
                td.append(cp(dqk[:, 2 * blk + i, :], ps, t, E=(S if i else None)))
                return td[-1]
            items += fm_items(hp, 512, win[l, 6 + blk], put, th, U)

        pipeline(items, 1)
        t = tt(G1, G1, v3(row(f"gb_{l}"), 4), ALU.add, tg)
        ta = ts(SPx[:, :, 0:4], G1[:, :, 4:8], -1.0, ALU.mult, t)
        tb = cp(SPx[:, :, 4:12], G1[:, :, 8:16], t)
        tsp = softplus(Lc, SPx, e1, u1, d1, ta, tb)
        dts = v3(small[0][:, 0:32], 4)
        td_ = cp(dts, Lc[:, :, 4:12], tsp)
        tA_ = act(small[1][:, 0:32], row(f"al_{l}"), ACT.Exp)
        t1 = ts(X[:, :, 0:4], Lc[:, :, 0:4], -1.0, ALU.mult, tsp)
        t2 = stt(X[:, :, 4:12], Lc[:, :, 4:12], -1.0, v3(small[1][:, 0:32], 4), ALU.mult, ALU.mult, tsp, tA_)
        b = banks.take()
        PE.wait(t1, t2, *b.w)
        mm(b.ap[:, 0:48], K["LE"], X.rearrange("p a b -> p (a b)"))
        mm(b.ap[:, 48:96], K["one"], X.rearrange("p a b -> p (a b)"))
        for i in range(4):
            for m in range(i + 1):
                p = mm(b.ap[:, 96 + 4 * i:100 + 4 * i], K["LE"] if m == i else K["one"], X[:, m, 0:4],
                       start=(m == 0), stop=(m == i), inc=(i == 3 and m == 3))
        t1 = cp(Lc, v3(b.ap[:, 0:48], 4), p, td_, t1, t2)
        t2 = cp(TOT, v3(b.ap[:, 48:96], 4), p)
        t3 = cp(Bg, v3(b.ap[:, 96:112], 4), p)
        b.free(t3)
        tcc = tt(cc, G1[:, :, 0:4], Bg, ALU.subtract, t3)
        b = banks.take()
        PE.wait(tcc, *b.w)
        for i in range(4):
            p = tr(b.ap[0:4, i * 128:(i + 1) * 128], cc[:, i, :], inc=(i == 3))
        t = cp(crow[0:4, :], b.ap[0:4, :], p, PE.now())
        b.free(t)
        tm = V(lambda h: h.tensor_tensor_scan(Mrow[0:4, :], crow[0:4, :], crow[0:4, :], 0.0, ALU.max, ALU.max), t)
        b = banks.take()
        PE.wait(tm, *b.w)
        for i in range(4):
            p = tr(b.ap[:, 4 * i:4 * i + 4], Mrow[0:4, i * 128:(i + 1) * 128], inc=(i == 3))
        t = tt(mt, Bg, v3(b.ap[:, 0:16], 4), ALU.add, p)
        b.free(t)
        tem = act(em, mt, ACT.Exp, t, scale=-1.0)
        snap(f"X{l}", X)
        snap(f"Mrow{l}", Mrow[0:4, :])

        Sd = [v3(tA, 4), v3(tB, 4)]
        E = [tC[:, 0:512], tC[:, 512:1024]]
        dg = [tC[:, 1024:1152], tC[:, 1152:1280]]
        Er, dgr, Sdr = [None, None], [None, None], [None, None]
        PE.wait(*tq, *tv, ti_)
        cnt = 0
        tY = []
        for h in range(4):
            bm = banks.take()
            pm = mm(bm.ap[:, :], sel[0:4, h * 128:(h + 1) * 128], Mrow[0:4, :], *bm.w, inc=True)
            r0 = (h % 2) * 64
            qh, kh = qk[r0:r0 + 64, h // 2, :], qk[r0:r0 + 64, 2 + h // 2, :]
            sd = Sd[h % 2]
            got = []
            for si in range(4):
                s0 = si * 128
                x = cnt % 2
                cnt += 1
                t = tt(dg[x], bm.ap[:, s0:s0 + 128], K["NEGU"], ALU.add, pm, dgr[x])
                t1 = act(E[x][:, s0:s0 + 128], dg[x], ACT.Exp, t, Er[x], bias=cc[:, si, h:h + 1], scale=-1.0)
                dgr[x] = t1
                if si < 3:
                    t1 = act(E[x][:, s0 + 128:512], bm.ap[:, s0 + 128:512], ACT.Exp, pm, Er[x],
                             bias=cc[:, si, h:h + 1], scale=-1.0)
                b = banks.take()
                p = mm(b.ap[:, s0:512], kh[:, s0:s0 + 128], qh[:, s0:512], *b.w, inc=True)
                t = stt(sd[:, si, s0:512], b.ap[:, s0:512], 0.125, E[x][:, s0:512], ALU.mult, ALU.mult,
                        p, t1, Sdr[h % 2])
                b.free(t)
                Er[x] = t
                got.append(t)
            bm.free(t1, got[-1])
            b = banks.take()
            PE.wait(*b.w)
            for ti in range(4):
                for si in range(ti + 1):
                    p = mm(b.ap[:, ti * 65:ti * 65 + 65], sd[:, si, ti * 128:(ti + 1) * 128], V1[:, si, h, :],
                           got[si], start=(si == 0), stop=(si == ti), inc=(si == ti))
            Sdr[h % 2] = p
            o = v3(b.ap[:, 0:260], 4)
            den = small[2 + h % 2][:, 0:4].unsqueeze(2)
            t = act(den, o[:, :, 64:65], ACT.Abs, p, *(tY[-2:-1]))
            t = tt(den, den, em[:, :, h:h + 1], ALU.max, t, tem)
            t = rcp(den, den, t)
            t = tt(Y[:, :, h * 64:h * 64 + 64], o[:, :, 0:64], den.to_broadcast([128, 4, 64]), ALU.mult, t)
            b.free(t)
            tY.append(t)
        snap(f"hm{l}", Y[:, :, 0:256])
        mof = mo.rearrange("p a b -> p (a b)")
        t = act(mof, mof, ACT.Tanh, *tv, scale=0.5)
        t = ts(mof, mof, 0.5, ALU.mult, t, s2=0.5, op1=ALU.add)
        Ym = Y[:, :, 0:256].rearrange("p a (g w) -> p a g w", g=4)
        tym = rms_tok(Ym, 4, 64, v4(tC[:, 0:1024], 4, 4), v3(small[4][:, 0:16], 4),
                      v3(row(f"mn_{l}"), 4), mo.rearrange("p a (g w) -> p a g w", g=4), t, *tY)
        snap(f"ym{l}", Y[:, :, 0:256])

        XS, XD = v3(hTf[:, 0:2048], 4), v3(hTf[:, 2048:4096], 4)
        cvt = [tB[:, 0:512], tB[:, 512:1024]]
        tcv = []
        for i in range(8):
            a = cvt[i % 2]
            w = coff[f"cw_{l}"][0] + 4 * i
            o = xbc[:, i, :]
            t = ts(a, o[:, 0:512], cols[:, w:w + 1], ALU.mult, *tx, tzero, tcv[-2] if i > 1 else None,
                   s2=col(f"cb_{l}", i), op1=ALU.add)
            for j in range(1, 4):
                t = stt(a, o[:, j:j + 512], cols[:, w + j:w + j + 1], a, ALU.mult, ALU.add, t)
            tcv.append(silu(o[:, 3:515], a, o[:, 3:515], t))
        txs = transposes(lambda n: xbc[:, n // 4, 3 + (n % 4) * 128:3 + (n % 4) * 128 + 128],
                         lambda n: XS[:, :, (n // 4) * 128:(n // 4) * 128 + 128], 16, 128, *tcv)
        snap(f"XS{l}", XS)
        txd = None
        for i in range(4):
            txd = tt(XD[:, i, :].rearrange("p (h c) -> p h c", h=8), XS[:, i, :].rearrange("p (h c) -> p h c", h=8),
                     dts[:, i, :].unsqueeze(2).to_broadcast([128, 8, 64]), ALU.mult, *txs)
        bia = al(16 * 8)
        bi = {}
        tb_ = None
        for si in range(4):
            for ti in range(si, 4):
                a = bia[:, (si * 4 + ti) * 8:(si * 4 + ti) * 8 + 8]
                bi[si, ti] = a
                if ti == si:
                    tb_ = ts(a, Lc[:, si, 4:12], -1.0, ALU.mult, t1)
                else:
                    tb_ = tt(a, bi[si, ti - 1], TOT[:, ti - 1, 4:12], ALU.add, tb_)
        CB = v3(xbc.rearrange("p a b -> p (a b)")[:, 0:2048], 4)
        Es = [v3(tB, 4), v3(tA, 4)]
        dg2 = [tC[:, 1024:1536], tC[:, 1536:2048]]
        tEr, tdg = [[PE.now(), V.now(), *txs]] * 2, [None, None]
        tEr = list(tEr)
        tCB, pv_last = None, None
        for h in range(8):
            g = h // 4
            if h % 4 == 0:
                tCB = []
                for si in range(4):
                    s0 = si * 128
                    b = banks.take()
                    p = mm(b.ap[:, s0:512], xbc[:, 4 + g, 3 + s0:3 + s0 + 128], xbc[:, 6 + g, 3 + s0:515],
                           *tcv, *b.w, inc=True)
                    e = cp(CB[:, si, s0:512], b.ap[:, s0:512], p, V.now(), E=(S if si % 2 else None))
                    b.free(e)
                    tCB.append(e)
            bl = banks.take()
            PE.wait(*bl.w)
            for i in range(4):
                pl = mm(bl.ap[:, i * 128:(i + 1) * 128], X[:, i, 4 + h:5 + h].to_broadcast([128, 128]), K["LE"],
                        inc=(i == 3))
            x = h % 2
            Eh = Es[x]
            t = tt(v3(dg2[x], 4), v3(bl.ap[:, :], 4), K["NEGU"].unsqueeze(1).to_broadcast([128, 4, 128]),
                   ALU.subtract, pl, tdg[x])
            tl = t
            got = []
            for si in range(4):
                s0 = si * 128
                t1 = act(Eh[:, si, s0:s0 + 128], dg2[x][:, s0:s0 + 128], ACT.Exp, tl, tEr[x], tb_,
                         bias=bi[si, si][:, h:h + 1])
                tdg[x] = t1
                for ti in range(si + 1, 4):
                    t1 = act(Eh[:, si, ti * 128:ti * 128 + 128], bl.ap[:, ti * 128:ti * 128 + 128], ACT.Exp, pl,
                             bias=bi[si, ti][:, h:h + 1])
                got.append(tt(Eh[:, si, s0:512], Eh[:, si, s0:512], CB[:, si, s0:512], ALU.mult, t1, *tCB))
            bl.free(t1, tl)
            b = banks.take()
            PE.wait(*b.w, txd)
            for ti in range(4):
                for si in range(ti + 1):
                    p = mm(b.ap[:, ti * 64:ti * 64 + 64], Eh[:, si, ti * 128:(ti + 1) * 128],
                           XD[:, si, h * 64:h * 64 + 64], got[si], start=(si == 0), stop=(si == ti), inc=(si == ti))
            tEr[x] = p
            t = stt(Y[:, :, 256 + h * 64:320 + h * 64], XS[:, :, h * 64:h * 64 + 64], row(f"D_{l}")[:, h:h + 1],
                    v3(b.ap[:, 0:256], 4), ALU.mult, ALU.add, p)
            b.free(t)
        snap(f"ssd{l}", Y[:, :, 256:768])
        ty = None
        for i in range(4):
            tmp = tC[:, (i % 2) * 512:(i % 2) * 512 + 512]
            ty = silu(z[:, i, :], z[:, i, :], tmp, *tz, tym, ty)
            ty = tt(Y[:, i, 256:768], Y[:, i, 256:768], z[:, i, :], ALU.mult, ty, t)
        tys = rms_tok(Y[:, :, 256:768].rearrange("p a (g w) -> p a g w", g=2), 2, 256, v4(tA, 4, 2),
                      v3(small[5][:, 0:8], 4), v3(row(f"sn_{l}"), 2), None, ty, PE.now())
        snap(f"ys{l}", Y[:, :, 256:768])

        barrier()
        lam = small[6]
        lr = row(f"lam_{l}")
        t = tt(tC[:, 0:32], lr[:, 0:32], lr[:, 32:64], ALU.mult)
        t = tt(tC[:, 32:64], lr[:, 64:96], lr[:, 96:128], ALU.mult, t)
        t = V(lambda h: h.tensor_reduce(lam[:, 0:2], v3(tC[:, 0:64], 2), AX, ALU.add), t)
        t = act(lam[:, 2:4], lam[:, 0:2], ACT.Exp, t)
        t = tt(lam[:, 4:5], lam[:, 2:3], lam[:, 3:4], ALU.subtract, t)
        tlam = ts(lam[:, 5:6], lam[:, 4:5], lam_init, ALU.add, t)
        rs, sq = hTf[:, 0:2048], hTf[:, 2048:4096]
        tn = []
        for i in range(4):
            s = act(sq[:, i * 512:(i + 1) * 512], dqk[:, i, :], ACT.Square, *td)
            b = banks.take()
            p = mm(b.ap[:, :], K["b32"], sq[:, i * 512:(i + 1) * 512], s, *b.w, inc=True)
            r = rs[:, i * 512:(i + 1) * 512]
            t = ts(r, b.ap[:, :], EPS, ALU.add, p)
            b.free(t)
            t = rcp(r, r, t)
            t = act(r, r, ACT.Sqrt, t)
            tn.append(stt(dqk[:, i, :], dqk[:, i, :], col(f"qw_{l}" if i < 2 else f"kw_{l}"), r, ALU.mult, ALU.mult, t))
        snap(f"dqk{l}", dqk)
        Lg = [[tA[:, (2 * i + j) * 512:(2 * i + j) * 512 + 512] for j in range(2)] for i in range(2)]
        Aw = [tB[:, i * 512:i * 512 + 512] for i in range(2)]
        AT = [tB[:, 1024 + i * 512:1536 + i * 512] for i in range(2)]
        st = small[8:10]
        tLr, tAr, tATr = [None, None], [None, None], [None, None]
        PE.wait(*tn, *tdv)
        cnt = 0
        tyd = None
        for h in range(4):
            for ti in range(4):
                x = cnt % 2
                cnt += 1
                n = (ti + 1) * 128
                ex = []
                m = st[x]
                for c in range(2):
                    r0 = (h % 2) * 64 + c * 32
                    b = banks.take()
                    p = mm(b.ap[:, 0:n], dqk[r0:r0 + 32, h // 2, ti * 128:n], dqk[r0:r0 + 32, 2 + h // 2, 0:n],
                           *b.w, inc=True)
                    L = Lg[x][c]
                    t = stt(L[:, 0:n], b.ap[:, 0:n], 32.0 ** -0.5, bias4[:, h, 512 - n:512], ALU.mult, ALU.add,
                            p, tLr[x])
                    b.free(t)
                    t = V(lambda h_, L=L, c=c, n=n, m=m: h_.reduce_max(m[:, c:c + 1], L[:, 0:n], AX), t)
                    t = ts(m[:, 2 + c:3 + c], m[:, c:c + 1], -1.0, ALU.mult, t)
                    ex.append(act(L[:, 0:n], L[:, 0:n], ACT.Exp, t, bias=m[:, 2 + c:3 + c], acc=m[:, 4 + c:5 + c]))
                t = rcp(m[:, 6:8], m[:, 4:6], *ex)
                t = tt(m[:, 8:9], m[:, 7:8], lam[:, 5:6], ALU.mult, t, tlam)
                t = ts(Lg[x][1][:, 0:n], Lg[x][1][:, 0:n], m[:, 8:9], ALU.mult, t)
                t = stt(Aw[x][:, 0:n], Lg[x][0][:, 0:n], m[:, 6:7], Lg[x][1][:, 0:n], ALU.mult, ALU.subtract, t, tAr[x])
                tLr[x] = t
                b = banks.take()
                for si in range(ti + 1):
                    p = tr(b.ap[:, si * 128:si * 128 + 128], Aw[x][:, si * 128:si * 128 + 128], t, *b.w, inc=(si == ti))
                tAr[x] = p
                t = cp(AT[x][:, 0:n], b.ap[:, 0:n], p, tATr[x], E=S)
                b.free(t)
                b = banks.take()
                for si in range(ti + 1):
                    p = mm(b.ap[:, 0:64], AT[x][:, si * 128:si * 128 + 128], dvt[:, si, h * 64:h * 64 + 64], t, *b.w,
                           start=(si == 0), stop=(si == ti), inc=(si == ti))
                tATr[x] = p
                tyd = cp(Y[:, ti, 768 + h * 64:832 + h * 64], b.ap[:, 0:64], p)
                b.free(tyd)
        snap(f"od{l}", Y[:, :, 768:1024])
        Yd = Y[:, :, 768:1024].rearrange("p a (g w) -> p a g w", g=4)
        tyd = rms_tok(Yd, 4, 64, v4(tC[:, 0:1024], 4, 4), v3(small[7][:, 0:16], 4),
                      row(f"sl_{l}").unsqueeze(1).to_broadcast([128, 4, 64]), 1.0 - lam_init, tyd)
        snap(f"Y{l}", Y)
        dst = parts(hTf, qkf)
        U = Units(tAB, 1024)
        ty = [fm_parts(lambda i, k=k: Y[:, i, k * 128:(k + 1) * 128], dst(k), V.now()) for k in range(8)]
        out_w(A["wout"], l, None, dst, ty, U)

    def out_w(wout, l, gain, src, dep, U):
        items = []
        for blk in range(4):
            def put(i, ps, t, blk=blk):
                k = 2 * blk + i
                if gain is None:
                    e = tt(xT[:, k, :], ps, xT[:, k, :], ALU.add, t)
                else:
                    e = stt(xT[:, k, :], ps, gain(k), xT[:, k, :], ALU.mult, ALU.add, t)
                stat_add(k, xT[:, k, :], e)
                return e
            items += fm_items(src, 512, wout[l, blk], put, dep, U)
        pipeline(items, len(U.hi) // 2)

    def modulation():
        reset()
        barrier()
        cs, tmp = v3(al(16), 8), al(16)
        t = silu(cs.rearrange("p a b -> p (a b)"), col("c", 0, 16), tmp)
        MR = [al(512), al(512)]
        r = [None, None]
        bt = banks.take()
        PE.wait(t, *bt.w)
        for j in range(12):
            b = banks.take()
            for half in range(2):
                s = load(A["wmod"][j * 2 + half])
                w4 = v3(s.ap, 4)
                for k in range(4):
                    kk = half * 4 + k
                    p = mm(b.ap[0:2, :], cs[:, kk, :], w4[:, k, :], s.t, *b.w, start=(kk == 0), stop=(kk == 7),
                           inc=(k == 3))
                done(s, p)
            e = cp(MR[j % 2][0:2, :], b.ap[0:2, :], p, r[j % 2], E=(S if j % 2 else None))
            b.free(e)
            for i in range(4):
                q = 4 * j + i
                r[j % 2] = tr(bt.ap[:, 2 * q:2 * q + 2], MR[j % 2][0:2, i * 128:(i + 1) * 128], e, inc=(i == 3))
        t = tt(MOD, v3(bt.ap[:, 0:96], 48), col("bmod", 0, 48).unsqueeze(2).to_broadcast([128, 48, 2]), ALU.add,
               r[1], r[0])
        bt.free(t)
        stt(A1.unsqueeze(2), MOD[:, 8:16, 0:1], 1.0, col("norm1", 0, 8).unsqueeze(2), ALU.add, ALU.mult, t)
        stt(A2.unsqueeze(2), MOD[:, 32:40, 0:1], 1.0, col("norm2", 0, 8).unsqueeze(2), ALU.add, ALU.mult, t)
        stt(Ac.unsqueeze(2), MOD[:, 8:16, 1:2], 1.0, col("norm1", 0, 8).unsqueeze(2), ALU.add, ALU.mult, t)
        snap("MOD", MOD)

    def conv2_l2(dst, tile, n, tmp, tmp2, ones_norm, scale, wts, tpad):
        w = coff["cw2"][0] + 4 * tile
        t = ts(tmp, wts[:, 0:n], cols[:, w:w + 1], ALU.mult, tpad)
        for j in range(1, 4):
            t = stt(tmp, wts[:, j:j + n], cols[:, w + j:w + j + 1], tmp, ALU.mult, ALU.add, t)
        t = silu(dst, tmp, tmp2, t)
        if not ones_norm:
            return t
        s = act(tmp, dst, ACT.Square, t)
        b = banks.take()
        p = mm(b.ap[:, 0:n], K["one"], tmp, s, *b.w, inc=True)
        t = ts(tmp, b.ap[:, 0:n], EPS, ALU.add, p)
        b.free(t)
        t = rcp(tmp, tmp, t)
        t = act(tmp, tmp, ACT.Sqrt, t)
        return stt(dst, dst, scale, tmp, ALU.mult, ALU.mult, t)

    def delta(nt, kT, Kt, Vt, qT, ab, tab, Sst, O, dep):
        w8 = lambda: v3(al(8 * nt), nt)
        a, beta, x = w8(), w8(), w8()
        e, u, d = w8(), w8(), w8()
        nb, eg, bg, tail, etot = w8(), w8(), w8(), w8(), w8()
        for i in range(nt):
            t = tt(a[:, i, :], ab[:, i, 0:8], row("dtb2"), ALU.add, tab)
        t = softplus(x, a, e, u, d, t)
        t2 = act(d[:, 0, :], row("al2"), ACT.Exp, t)
        for i in range(nt):
            tx = stt(x[:, i, :], x[:, i, :], -1.0, d[:, 0, :], ALU.mult, ALU.mult, t, t2)
        bb = ab[:, :, 8:16]
        t = act(e, bb, ACT.Abs, tx, tab)
        t = act(e, e, ACT.Exp, t, scale=-1.0)
        t = ts(e, e, 1.0, ALU.add, t)
        t = rcp(e, e, t)
        t2 = ts(beta, bb, 0.0, ALU.min, t)
        t2 = act(beta, beta, ACT.Exp, t2)
        t = tt(beta, beta, e, ALU.mult, t2)
        tnb = ts(nb, beta, -1.0, ALU.mult, t)
        b = banks.take()
        PE.wait(tx, *b.w)
        n8 = 8 * nt
        for i in range(nt):
            for dr in range(2):
                c = slice(8 * i + 4 * dr, 8 * i + 4 * dr + 4)
                xs = x[:, i, 4 * dr:4 * dr + 4]
                mm(b.ap[:, c], K["LE" if dr == 0 else "GE"], xs)
                mm(b.ap[:, n8 + c.start:n8 + c.stop], K["GT" if dr == 0 else "LT"], xs)
        p = mm(b.ap[:, 2 * n8:3 * n8], K["one"], x.rearrange("p a b -> p (a b)"), inc=True)
        t1 = act(eg, v3(b.ap[:, 0:n8], nt), ACT.Exp, p)
        t2 = act(tail, v3(b.ap[:, n8:2 * n8], nt), ACT.Exp, p)
        t3 = act(etot, v3(b.ap[:, 2 * n8:3 * n8], nt), ACT.Exp, p)
        b.free(t3)
        tbg = tt(bg, beta, eg, ALU.mult, t1, tnb)
        snap(f"x2_{nt}", x)
        part = lambda m, o: [m[:, o + 128 * q:o + 128 * q + 128] for q in range(8)]
        XB, kbg, vb, kt = (part(hTf, 1024 * q) for q in range(4))
        P_, Tb = part(b4f, 0), part(b4f, 1024)
        Ex = [al(256) for _ in range(8)]
        wT, uu = part(al(1024), 0), part(al(1024), 0)
        W = part(al(1024), 0) if qT is not None else None
        LB = [al(384) for _ in range(8)]
        Yb = [al(64) for _ in range(8)]
        barrier()
        J = range(8)
        for step in range(nt):
            tile = [step if j < 4 else nt - 1 - step for j in J]
            sc = lambda m, j: m[:, tile[j], j:j + 1]
            cs = lambda j: slice(tile[j] * 128, tile[j] * 128 + 128)
            hh = lambda j: j % 4
            tE, tPb, tP, tkb, tvb, tkt, tW = ({} for _ in range(7))
            for j in J:
                f = j < 4
                t = ts(XB[j], K["GT"] if f else K["LT"], sc(x, j), ALU.mult, PE.now() if j == 0 else None)
                b = banks.take()
                mm(b.ap[:, 0:128], K["LE"] if f else K["GE"], XB[j], t, *b.w)
                p = mm(b.ap[:, 128:256], XB[j], K["LE"] if f else K["GE"], inc=True)
                t = act(Ex[j], b.ap[:, 0:256], ACT.Exp, p, V.now(), G.now())
                b.free(t)
                m0 = CO["GT"] if f else CO["LT"]
                tE[j] = G(lambda h, j=j, m0=m0: h.tensor_tensor(Ex[j], Ex[j], kst[:, m0:m0 + 256], ALU.mult), t)
            for j in J:
                kh = kT[:, hh(j), cs(j)]
                b = banks.take()
                p = mm(b.ap[:, 0:128], kh, kh, *b.w, inc=True)
                if qT is not None:
                    p = mm(b.ap[:, 128:256], kh, qT[:, hh(j), cs(j)], inc=True)
                tP[j] = t = stt(P_[j], b.ap[:, 0:128], sc(nb, j), Ex[j][:, 0:128], ALU.mult, ALU.mult, p, tE[j])
                if qT is not None:
                    t = tt(W[j], b.ap[:, 128:256], Ex[j][:, 128:256], ALU.mult)
                    tW[j] = t
                b.free(t)
                tPb[j] = tt(LB[j][:, 0:128], P_[j], K["bd"], ALU.mult, tP[j], E=G)
                kt_, vt_ = Kt[:, tile[j], hh(j) * 128:hh(j) * 128 + 128], Vt[:, tile[j], hh(j) * 128:hh(j) * 128 + 128]
                tkb[j] = ts(kbg[j], kt_, sc(bg, j), ALU.mult, E=G)
                tvb[j] = ts(vb[j], vt_, sc(beta, j), ALU.mult, E=G)
                tkt[j] = ts(kt[j], kt_, sc(tail, j), ALU.mult, E=G)
            tL, tT = {}, {}
            for j in J:
                b = banks.take()
                p = tr(b.ap[:, 0:128], LB[j][:, 0:128], tPb[j], *b.w, inc=True)
                tL[j] = cp(LB[j][:, 128:256], b.ap[:, 0:128], p, E=S)
                tT[j] = tt(LB[j][:, 256:384], b.ap[:, 0:128], ident, ALU.add, p, tL[j])
                b.free(tL[j], tT[j])
            for lev in range(6):
                for j in J:
                    b = banks.take()
                    L = LB[j]
                    if lev == 5:
                        p = mm(b.ap[:, 256:384], L[:, 0:128], L[:, 256:384], tL[j], tT[j], *b.w, inc=True)
                    else:
                        hi = 256 if lev == 0 else 384
                        mm(b.ap[:, 128:hi], L[:, 0:128], L[:, 128:hi], tL[j], tT[j], *b.w)
                        p = mm(b.ap[:, 0:128], L[:, 128:256], L[:, 0:128], inc=True)
                        tL[j] = cp(L[:, 0:256], b.ap[:, 0:256], p, E=S)
                    if lev:
                        tT[j] = tt(L[:, 256:384], b.ap[:, 256:384], L[:, 256:384], ALU.add, p, tL[j])
                    b.free(tL[j], tT[j])
            t2 = {}
            for j in J:
                TT = LB[j][:, 256:384]
                b = banks.take()
                tr(b.ap[:, 0:128], TT, tT[j], *b.w)
                lo, hi = (0, 64) if j < 4 else (64, 0)
                p = mm(b.ap[lo:lo + 64, 128:192], P_[j][hi:hi + 64, lo:lo + 64], TT[hi:hi + 64, hi:hi + 64], tP[j], inc=True)
                t1 = cp(Tb[j], b.ap[:, 0:128], p, E=S)
                t3 = cp(Yb[j][lo:lo + 64, :], b.ap[lo:lo + 64, 128:192], p, E=S)
                b.free(t1, t3)
                t2[j] = t3
            for j in J:
                TT = LB[j][:, 256:384]
                lo, hi = (0, 64) if j < 4 else (64, 0)
                b = banks.take()
                p = mm(b.ap[lo:lo + 64, 0:64], Tb[j][lo:lo + 64, lo:lo + 64], Yb[j][lo:lo + 64, :], t2[j], *b.w, inc=True)
                tT[j] = cp(TT[lo:lo + 64, hi:hi + 64], b.ap[lo:lo + 64, 0:64], p)
                b.free(tT[j])
            tu = {}
            for j in J:
                TT = LB[j][:, 256:384]
                b = banks.take()
                mm(b.ap[:, 0:128], kbg[j], TT, tT[j], tkb[j], tvb[j], *b.w)
                p = mm(b.ap[:, 128:256], TT, vb[j], inc=True)
                t1 = cp(wT[j], b.ap[:, 0:128], p, E=S)
                t3 = cp(uu[j], b.ap[:, 128:256], p, t1)
                b.free(t1, t3)
                tu[j] = [t1, t3]
            if step == 0:
                snap(f"LB_{nt}", LB[0])
                snap(f"LB4_{nt}", LB[4])
            tun, bq = {}, {}
            for j in J:
                b = banks.take()
                p = mm(b.ap[:, 0:128], wT[j], Sst[:, j, :], *tu[j], *b.w, dep, inc=True)
                tun[j] = stt(uu[j], b.ap[:, 0:128], -1.0, uu[j], ALU.mult, ALU.add, p)
                b.free(tun[j])
            for j in J:
                b = banks.take()
                PE.wait(*b.w, tun[j], tkt[j])
                p = mm(b.ap[:, 0:128], kt[j], uu[j], inc=(qT is None))
                if qT is not None:
                    mm(b.ap[:, 128:256], qT[:, hh(j), cs(j)], Sst[:, j, :])
                    p = mm(b.ap[:, 256:384], W[j], uu[j], tW[j], inc=True)
                t = stt(Sst[:, j, :], Sst[:, j, :], sc(etot, j), b.ap[:, 0:128], ALU.mult, ALU.add, p)
                dep = t
                if qT is not None:
                    o = O[:, tile[j], hh(j) * 128:hh(j) * 128 + 128]
                    t = stt(o, b.ap[:, 128:256], sc(eg, j), o, ALU.mult, ALU.add, p)
                    t = tt(o, b.ap[:, 256:384], o, ALU.add, t)
                b.free(t)

    CO = {n: i * 128 for i, n in enumerate(CONSTS)}

    def context():
        reset()
        barrier()
        kT = v3(al(4 * 256), 4)
        Kt, Vt = v3(al(1024), 2), v3(al(1024), 2)
        ab = v3(al(32), 2)
        mark = top[0]
        cT = v3(al(8 * 256), 8)
        ct = v3(al(2048), 2)
        t = misc(S, ct, A["ctx"].rearrange("(t p) d -> p t d", p=128))
        to_fm(ct, cT, 2, t, stats=True)
        hp = parts(hTf, al(4096), 256)
        U = Units(al(8192), 1024)
        th = norm_fm(cT, hp, lambda k: Ac[:, k:k + 1], 256, lambda k: MOD[:, k, 1:2])
        vT = v3(al(4 * 256), 4)
        raw = v3(al(8 * 260), 8)
        tmp = [al(256) for _ in range(4)]
        tz = V(lambda h: h.memset(raw, 0.0))
        tab = proj_small(hp, 2, 2, ab, th)
        tp = []
        items = []
        for blk in range(4):
            def put(i, ps, t, blk=blk):
                tp.append(cp(raw[:, 2 * blk + i, 2:258], ps, t, tz, E=(S if i else None)))
                return tp[-1]
            items += fm_items(hp, 256, A["win2"][2 + blk], put, th, U)
        pipeline(items, 2)
        tc = []
        V.wait(*tp)
        for i in range(4):
            tc.append(conv2_l2(kT[:, i, :], 4 + i, 256, tmp[0], tmp[1], True, 1.0, raw[:, i, :], tc[-1] if tc else None))
            tc.append(conv2_l2(vT[:, i, :], 8 + i, 256, tmp[2], tmp[3], False, 1.0, raw[:, 4 + i, :], tc[-1]))
        S.wait(*tc)
        tk = tok_from(kT, Kt, 2, tc) + tok_from(vT, Vt, 2, tc)
        t = V(lambda h: h.memset(ctxS, 0.0))
        barrier()
        top[0] = mark
        delta(2, kT, Kt, Vt, None, ab, tab, ctxS, None, [t] + tk)
        snap("ctxS", ctxS)

    def tok_from(src, dst, nt, dep):
        out = []
        for t in range(nt):
            b = banks.take()
            for i in range(4):
                p = tr(b.ap[:, i * 128:(i + 1) * 128], src[:, i, t * 128:(t + 1) * 128], *dep, *b.w, inc=(i == 3))
            e = cp(dst[:, t, :], b.ap[:, :], p, E=(S if t % 2 else None))
            b.free(e)
            out.append(e)
        return out

    def mixer2():
        reset()
        barrier()
        gate, poolT = v3(al(2048), 4), v3(al(2048), 4)
        ab = v3(al(64), 4)
        qkf2 = al(4096)
        qT, kT = v3(qkf2[:, 0:2048], 4), v3(qkf2[:, 2048:4096], 4)
        KVf = al(4096)
        Kt, Vt = v3(KVf[:, 0:2048], 4), v3(KVf[:, 2048:4096], 4)
        O = v3(al(2048), 4)
        mark = top[0]
        mTf = al(2048)
        mT = v3(mTf, 4)
        vT = v3(al(2048), 4)
        raw = v3(al(4 * 516), 4)
        ut = v3(al(2048), 4)
        tmp = [al(512) for _ in range(4)]
        U = Units(at(mark - 2048, 4096), 1024)
        hp = parts(hTf, KVf)
        th = norm_fm(xT, hp, lambda k: A1[:, k:k + 1], 512, lambda k: MOD[:, k, 0:1])
        tab = proj_small(hp, 4, 2, ab, th)
        items = []
        tg = []
        for half in range(2):
            def put(i, ps, t, half=half):
                tg.append(cp(gate[:, i, half * 256:half * 256 + 256], ps, t, E=S))
                return tg[-1]
            items += tok_items(hp, 4, A["win2"][6 + half], put, th, U)
        tu = []
        for half in range(2):
            def put(i, ps, t, half=half):
                tu.append(cp(ut[:, i, half * 256:half * 256 + 256], ps, t, E=S))
                return tu[-1]
            items += tok_items(hp, 4, A["win2"][8 + half], put, th, U)
        tz = V(lambda h: h.memset(raw, 0.0))
        pipeline(items, 1)
        tc = []
        for part, dst in enumerate((qT, kT, vT)):
            tp = []
            items = []
            for blk in range(2):
                def put(i, ps, t, blk=blk):
                    tp.append(cp(raw[:, 2 * blk + i, 2:514], ps, t, tz, tc[-1] if tc else None, E=(S if i else None)))
                    return tp[-1]
                items += fm_items(hp, 512, A["win2"][2 * part + blk], put, th, U)
            pipeline(items, 1)
            V.wait(*tp)
            for i in range(4):
                tc.append(conv2_l2(dst[:, i, :], 4 * part + i, 512, tmp[0], tmp[1], part < 2,
                                   128.0 ** -0.5 if part == 0 else 1.0, raw[:, i, :], tc[-1] if tc else None))
        tk = tok_from(kT, Kt, 4, tc) + tok_from(vT, Vt, 4, tc)
        for g in range(4):
            s = load(A["k_box"][g])
            bx = v3(s.ap, 4)
            b = banks.take()
            for t_ in range(4):
                p = mm(b.ap[:, :], ut[:, t_, g * 128:g * 128 + 128], bx[:, t_, :], s.t, *tu, *b.w, start=(t_ == 0),
                       stop=(t_ == 3), inc=(t_ == 3))
            done(s, p)
            e = cp(mT[:, g, :], b.ap[:, :], p, E=S)
            b.free(e)
            b = banks.take()
            p = mm(b.ap[:, :], poolw[:, g * 128:(g + 1) * 128], mT[:, g, :], e, *b.w, inc=True)
            e = ts(poolT[:, g, :], b.ap[:, :], col("psc", g), ALU.mult, p)
            b.free(e)
        snap("poolT", poolT)
        barrier()
        t = V(lambda h: h.memset(O, 0.0))
        top[0] = mark
        delta(4, kT, Kt, Vt, qT, ab, tab, ctxS, O, [t] + tk)
        barrier()
        snap("O", O)
        top[0] = mark
        tmp, sq = al(2048), al(2048)
        gf = gate.rearrange("p a b -> p (a b)")
        t = silu(gf, gf, tmp)
        ms = v3(al(16), 4)
        O4 = O.rearrange("p a (g w) -> p a g w", g=4)
        t = rms_tok(O4, 4, 128, v4(sq, 4, 4), ms, row("dn").unsqueeze(1).to_broadcast([128, 4, 128]),
                    gate.rearrange("p a (g w) -> p a g w", g=4), t)
        dst = parts(hTf, qkf2)
        U = Units(KVf, 1024)
        dep = [fm_parts(lambda i, k=k: O[:, i, k * 128:(k + 1) * 128], dst(k), t) for k in range(4)]
        dep += [split(*dst(4 + k), poolT[:, k, :]) for k in range(4)]
        out_w(A["wout2"], 0, lambda k: MOD[:, 16 + k, 0:1], dst, dep, U)
        snap("x2a", xT)

    def experts():
        reset()
        barrier()
        hh, hl = al(4096), al(4096)
        hp = parts(hh, hl)
        th = norm_fm(xT, hp, lambda k: A2[:, k:k + 1], 512, lambda k: MOD[:, 24 + k, 0:1], full=hT)
        snap("h2b", hT)
        ht = v3(al(4096), 4)
        th2 = []
        for i in range(4):
            for k0 in range(0, 8, 4):
                b = banks.take()
                for k in range(4):
                    p = tr(b.ap[:, k * 128:(k + 1) * 128], hT[:, k0 + k, i * 128:(i + 1) * 128], *th, *b.w, inc=(k == 3))
                e = cp(ht[:, i, k0 * 128:k0 * 128 + 512], b.ap[:, :], p, E=(S if k0 else None))
                b.free(e)
                th2.append(e)
        hd = nc.dram_tensor("h_scratch", [T, D], F32)
        t_h = misc(S, hd.ap().rearrange("(t p) d -> p t d", p=128), ht, *th2)
        lg = v3(al(64), 4)
        tl = proj_small(hp, 4, 3, lg, th)
        mx = v3(al(4), 4)
        t = V(lambda h: h.tensor_reduce(mx.squeeze(2) if False else mx[:, :, 0], lg, AX, ALU.max), tl)
        t = tt(lg, lg, mx.to_broadcast([128, 4, 16]), ALU.subtract, t)
        t = act(lg, lg, ACT.Exp, t)
        t = V(lambda h: h.tensor_reduce(mx[:, :, 0], lg, AX, ALU.add), t)
        t = rcp(mx, mx, t)
        t = tt(lg, lg, mx.to_broadcast([128, 4, 16]), ALU.mult, t)
        snap("aff", lg)
        b = banks.take()
        for i in range(4):
            p = tr(b.ap[0:16, i * 128:(i + 1) * 128], lg[:, i, :], t, *b.w, inc=(i == 3))
        wk = [al(512), al(512)]
        t = cp(wk[0][0:16, :], b.ap[0:16, :], p)
        b.free(t)
        vals = al(64)
        idx = memu[:, 0:64]
        for r in range(8):
            v8 = vals[0:16, 8 * r:8 * r + 8]
            a, bb = wk[r % 2][0:16, :], wk[(r + 1) % 2][0:16, :]
            t = V(lambda h, v8=v8, a=a: h.max(v8, a), t)
            t1 = V(lambda h, v8=v8, a=a, r=r: h.max_index(idx[0:16, 8 * r:8 * r + 8], v8, a), t)
            t = V(lambda h, v8=v8, a=a, bb=bb: h.match_replace(bb, v8, a, -1.0), t1)
        idd = nc.dram_tensor("idx_scratch", [1024], U32)
        vd = nc.dram_tensor("val_scratch", [1024], F32)
        t1 = misc(S, idd.ap().rearrange("(e c) -> e c", e=16), idx[0:16, :], t)
        t2 = misc(S, vd.ap().rearrange("(e c) -> e c", e=16), vals[0:16, :], t)
        ixT, vT = memu[:, 64:72], al(8)
        t1 = misc(S, ixT, idd.ap().rearrange("(j p) -> p j", p=128), t1, slow=True)
        t2 = misc(S, vT, vd.ap().rearrange("(j p) -> p j", p=128), t2, slow=True)
        ixf = al(8)
        tix = cp(ixf, ixT, t1)
        V.wait(t2)
        S.wait(t2)
        snap("ixf", ixf)
        iot = al(512)
        ti = G(lambda h: h.iota(iot, [[1, 512]], base=0, channel_multiplier=0, allow_small_or_imprecise_dtypes=True))
        piece = lambda i: (hh, hl)[i // 4][:, (i % 4) * 1024:(i % 4) * 1024 + 1024]
        xe = [piece(0), piece(1)]
        xeT = [v3(piece(2), 8), v3(piece(3), 8)]
        hid = [piece(4), piece(5)]
        hidT = [v3(piece(6), 8), v3(piece(7), 8)]
        ye = [al(1024) for _ in range(2)]
        oh = [al(512) for _ in range(2)]
        ex = [al(512) for _ in range(2)]
        exr = [None, None]
        xe_r, xeT_r, hid_r, hidT_r, ye_r = ([None, None] for _ in range(5))
        gs = [nc.alloc_semaphore(f"gather{i}") for i in range(8)]
        for pr in range(8):
            x = pr % 2
            G.wait(t_h, t1, xe_r[x])
            G.q.append(lambda pr=pr, x=x: nc.gpsimd.indirect_dma_start(
                xe[x], None, hd.ap(), bass.IndirectOffsetOnAxis(ap=ixT[:, pr:pr + 1], axis=0)).then_inc(gs[pr], 16))
            tgat = (gs[pr], 16)
            toh = ts(oh[x], iot, ixf[:, pr:pr + 1], ALU.is_equal, ti, tix, ye_r[x])
            tx = []
            for k0 in range(0, 8, 4):
                b = banks.take()
                for k in range(4):
                    p = tr(b.ap[:, k * 128:(k + 1) * 128], xe[x][:, (k0 + k) * 128:(k0 + k + 1) * 128], tgat, *b.w,
                           inc=(k == 3))
                e = cp(xeT[x][:, k0:k0 + 4, :], v3(b.ap[:, :], 4), p, xeT_r[x], E=(S if k0 else None))
                b.free(e)
                tx.append(e)
            xe_r[x] = p

            def wide(w, lhs, dep, half):
                b = banks.take()
                for e_ in range(2):
                    for kh in range(2):
                        s = load(A[w][(2 * pr + e_) * 4 + half * 2 + kh])
                        w4 = v3(s.ap, 4)
                        for k in range(4):
                            kk = kh * 4 + k
                            p = mm(b.ap[64 * e_:64 * e_ + 64, :], lhs[:, kk, 64 * e_:64 * e_ + 64], w4[:, k, :], s.t,
                                   *dep, *b.w, start=(kk == 0), stop=(kk == 7), inc=(k == 3))
                        done(s, p)
                return b, p
            th_ = []
            for half in range(2):
                bg, pg = wide("eg", xeT[x], tx, half)
                bu, pu = wide("eu", xeT[x], tx, half)
                e = ex[half]
                t = act(e, bg.ap[:, :], ACT.Tanh, pg, exr[half], scale=0.5)
                t = stt(e, e, 1.0, bg.ap[:, :], ALU.add, ALU.mult, t)
                bg.free(t)
                t = tt(hid[x][:, half * 512:half * 512 + 512], e, bu.ap[:, :], ALU.mult, t, pu, hid_r[x])
                bu.free(t)
                exr[half] = t
                th_.append(t)
            xeT_r[x] = pu
            tx = []
            for k0 in range(0, 8, 4):
                b = banks.take()
                for k in range(4):
                    p = tr(b.ap[:, k * 128:(k + 1) * 128], hid[x][:, (k0 + k) * 128:(k0 + k + 1) * 128], *th_, *b.w,
                           inc=(k == 3))
                e = cp(hidT[x][:, k0:k0 + 4, :], v3(b.ap[:, :], 4), p, hidT_r[x], E=(S if k0 else None))
                b.free(e)
                tx.append(e)
            hid_r[x] = p
            ty = []
            for half in range(2):
                bd, pd = wide("ed", hidT[x], tx, half)
                t = ts(ye[x][:, half * 512:half * 512 + 512], bd.ap[:, :], vT[:, pr:pr + 1], ALU.mult, pd, ye_r[x],
                       s2=0.5, op1=ALU.mult)
                bd.free(t)
                ty.append(t)
            hidT_r[x] = pd
            for k in range(8):
                b = banks.take()
                p = mm(b.ap[:, :], ye[x][:, k * 128:(k + 1) * 128], oh[x], *ty, toh, *b.w, inc=True)
                t = stt(xT[:, k, :], b.ap[:, :], MOD[:, 40 + k, 0:1], xT[:, k, :], ALU.mult, ALU.add, p)
                b.free(t)
                if pr == 7:
                    stat_add(k, xT[:, k, :], t)
            ye_r[x] = p

    def output():
        reset()
        barrier()
        hh, hl = al(4096), al(4096)
        t = norm_fm(xT, parts(hh, hl), lambda k: col("normf", k), 512, full=hT)
        ot = [al(1024) for _ in range(4)]
        for i in range(4):
            es = []
            for k0 in range(0, 8, 4):
                b = banks.take()
                for k in range(4):
                    p = tr(b.ap[:, k * 128:(k + 1) * 128], hT[:, k0 + k, i * 128:(i + 1) * 128], *t, *b.w, inc=(k == 3))
                e = cp(ot[i][:, k0 * 128:k0 * 128 + 512], b.ap[:, :], p, E=(S if k0 else None))
                b.free(e)
                es.append(e)
            misc(S, out_x[i * 128:(i + 1) * 128, :], ot[i], *es)

    def start():
        reset()
        barrier()
        tb = rel_table()
        for e in (V, PE):
            e.wait(tb)
        reset()
        barrier()
        xt0 = v3(al(4096), 4)
        t = misc(S, xt0, A["x"].rearrange("(t p) d -> p t d", p=128))
        to_fm(xt0, xT, 4, t, stats=True)

    stages = [modulation, context, start]
    for l in range(2):
        stages += [lambda l=l: ffn(2 * l, f"n1_{l}"), lambda l=l: snap(f"xa{l}", xT), lambda l=l: mixer(l),
                   lambda l=l: snap(f"xb{l}", xT), lambda l=l: ffn(2 * l + 1, f"n2_{l}"),
                   lambda l=l: snap(f"xc{l}", xT)]
    stages += [mixer2, experts, output]
    if isinstance(upto, int):
        stages = stages[:upto]
    else:
        stages = [s for i, s in enumerate(stages) if i in upto]
    for s in stages:
        s()
    SP.wait(*dma_all)
    SP.wait(*every())

    with nc.Block() as block:
        @block.sync
        def _(e):
            SP.run()

        @block.scalar
        def _(e):
            S.run()

        @block.vector
        def _(e):
            V.run()

        @block.gpsimd
        def _(e):
            G.run()

        @block.tensor
        def _(e):
            PE.run()
    return {e.name: len(e.q) for e in (PE, V, S, G, SP)}


def lay_out(i):
    f = lambda a: np.asarray(a)
    o = {}

    def blocks(w, nk, nc_):
        K_, N = w.shape
        a = w.reshape(K_ // (128 * nk), nk, 128, N // nc_, nc_).transpose(3, 0, 2, 1, 4)
        return a.reshape(-1, 128, nk * nc_)

    pairs = [("ffn1", 0), ("ffn2", 0), ("ffn1", 1), ("ffn2", 1)]
    o["wg"] = np.stack([blocks(f(i[n + "_w_gate"])[l], 8, 256) for n, l in pairs])
    o["wu"] = np.stack([blocks(f(i[n + "_w_up"])[l], 8, 256) for n, l in pairs])
    o["wd0"] = np.stack([blocks(f(i[n + "_w_down"])[l, 0:1536], 12, 128) for n, l in pairs])
    o["wd1"] = np.stack([blocks(f(i[n + "_w_down"])[l, 1536:], 10, 128) for n, l in pairs])
    w = f(i["w_in"])
    fm = np.concatenate([w[:, :, 0:512], w[:, :, 1544:2568], w[:, :, 2576:3088], w[:, :, 512:1024],
                         w[:, :, 1032:1544], w[:, :, 3088:3344]], 2)
    o["win"] = np.stack([blocks(fm[l], 8, 256) for l in range(2)])
    o["wout"] = np.stack([blocks(f(i["w_out"])[l], 8, 256) for l in range(2)])
    w2 = f(i["w_in_2"])[0]
    o["win2"] = blocks(np.concatenate([w2[:, 0:1536], w2[:, 1552:2576]], 1), 8, 256)
    o["wout2"] = blocks(f(i["w_out_2"])[0], 8, 256)[None]
    o["wmod"] = blocks(f(i["w_mod_2"])[0], 4, 512)
    for n, k in (("eg", "w_gate_2"), ("eu", "w_up_2"), ("ed", "w_down_2")):
        w = f(i[k])[0]
        o[n] = w.reshape(16, 2, 4, 128, 2, 512).transpose(0, 4, 1, 3, 2, 5).reshape(64, 128, 2048)
    k8 = lambda a: a.reshape(8, 128, -1).transpose(1, 0, 2).reshape(128, -1)
    sm = [np.concatenate([w_[:, 1024:1032], w_[:, 2568:2576]], 1) for w_ in f(i["w_in"])]
    o["smallw"] = np.concatenate([k8(sm[0]), k8(sm[1]), k8(w2[:, 1536:1552]), k8(f(i["w_router_2"])[0])], 1)
    o["poolw"] = f(i["pool_w_2"])[0].transpose(1, 0, 2).reshape(128, 512)
    c8 = lambda a: a.reshape(-1, 128).T
    cols, rows = {}, {}
    for l in range(2):
        cols[f"n1_{l}"] = c8(f(i["ffn1_norm_w"])[l])
        cols[f"nm_{l}"] = c8(f(i["mix_norm_w"])[l])
        cols[f"n2_{l}"] = c8(f(i["ffn2_norm_w"])[l])
        cols[f"cw_{l}"] = f(i["ssm_conv_w"])[l].reshape(4, 8, 128).transpose(2, 1, 0).reshape(128, 32)
        cols[f"cb_{l}"] = c8(f(i["ssm_conv_b"])[l])
        cols[f"qw_{l}"] = np.tile(f(i["diff_q_norm_w"])[l].reshape(64), 2)[:, None]
        cols[f"kw_{l}"] = np.tile(f(i["diff_k_norm_w"])[l].reshape(64), 2)[:, None]
        gb = np.concatenate([f(i["mlstm_gate_bias"])[l].reshape(8), f(i["ssm_dt_bias"])[l]])
        rows[f"gb_{l}"] = np.tile(gb, 4)
        rows[f"al_{l}"] = np.tile(f(i["ssm_A_log"])[l], 4)
        rows[f"mn_{l}"] = f(i["mlstm_norm_w"])[l]
        rows[f"sn_{l}"] = f(i["ssm_norm_w"])[l]
        rows[f"D_{l}"] = f(i["ssm_D"])[l]
        rows[f"sl_{l}"] = f(i["diff_subln_w"])[l]
        rows[f"lam_{l}"] = f(i["diff_lambda"])[l].reshape(128)
    cols["norm1"] = c8(f(i["norm1_2"])[0])
    cols["norm2"] = c8(f(i["norm2_2"])[0])
    cols["normf"] = c8(f(i["norm_f_2"]))
    cols["cw2"] = f(i["conv_w_2"])[0].reshape(4, 12, 128).transpose(2, 1, 0).reshape(128, 48)
    cols["psc"] = c8(f(i["pool_scale_2"])[0])
    cols["c"] = np.stack([c8(f(i["c_2"])[0]), c8(f(i["c_ctx_2"]))], 2).reshape(128, 16)
    cols["bmod"] = c8(f(i["b_mod_2"])[0])
    rows["al2"] = f(i["a_log_2"])[0].reshape(8)
    rows["dtb2"] = f(i["dt_bias_2"])[0].reshape(8)
    rows["dn"] = f(i["dn_norm_2"])[0]
    o["cols"] = np.concatenate([cols[n] for n, _ in COLS], 1)
    o["rows"] = np.tile(np.concatenate([rows[n] for n, _ in ROWS])[None], (128, 1))
    o["rel_bias"] = f(i["rel_bias"])
    o["x"] = f(i["x"])[0]
    o["ctx"] = f(i["ctx_2"])[0]
    o["k_const"], o["k_sel"], o["k_oh"], o["k_neg"], o["k_box"] = const_arrays()
    return {n: np.ascontiguousarray(a) for n, a in o.items()}


def kernel(**inputs):
    import concourse.bacc as _bacc
    from concourse.bass_utils import run_bass_kernel_spmd as _run

    nc = _bacc.Bacc("TRN2", target_bir_lowering=False, num_devices=1)
    arrays = {"in_" + n: a for n, a in lay_out(inputs).items()}
    A = {n[3:]: nc.dram_tensor(n, a.shape, mybir.dt.from_np(a.dtype), kind="ExternalInput").ap()
         for n, a in arrays.items()}
    out = nc.dram_tensor("out_x", (T, D), F32, kind="ExternalOutput").ap()
    build(nc, A, out)
    r = _run(nc, [arrays], core_ids=[0])
    return r.results[0]["out_x"].reshape(1, T, D)
```

```python
import numpy as np

import concourse.bass as bass
import concourse.mybir as mybir
from concourse.alu_op_type import AluOpType as ALU

F32 = mybir.dt.float32
FR = mybir.dt.float32r
U32 = mybir.dt.uint32
ACT = mybir.ActivationFunctionType
AX = mybir.AxisListType.X

T = 512
D = 1024
FF = 2816
NF = FF // 128
BIG = 1.0e30
MEM_AT = 16512
EPS = 1e-6
NSLOT = 4
SLOT = 2048

CONSTS = ["ident", "one", "b32", "GT", "LE", "LT", "GE", "NEGU", "bd"]


def const_arrays():
    p = np.arange(128)[:, None]
    j = np.arange(128)[None, :]
    c = {
        "ident": p == j, "one": np.ones((128, 128)), "b32": (p // 32 == j // 32) / 32.0,
        "GT": p > j, "LE": p <= j, "LT": p < j, "GE": p >= j,
        "NEGU": np.where(p <= j, 0.0, BIG), "bd": p // 64 == j // 64,
    }
    k = np.concatenate([np.asarray(c[n], np.float32) for n in CONSTS], 1)
    sel = np.zeros((4, 4, 128), np.float32)
    for h in range(4):
        sel[h, h] = 1.0
    rel = 511 - np.arange(640)
    n = np.maximum(rel, 0)
    nf = np.maximum(n, 1).astype(np.float32)
    large = 16 + (np.log(nf / np.float32(16)) / np.float32(np.log(8.0)) * np.float32(16)).astype(np.int32)
    bucket = np.where(n < 16, n, np.minimum(large, 31))
    oh = ((bucket[None, :] == np.arange(32)[:, None]) & (rel >= 0)[None, :]).astype(np.float32)
    neg = np.tile(np.where(rel < 0, np.float32(-BIG), np.float32(0.0)), (128, 1))
    box = np.zeros((4, 512, 512), np.float32)
    for g, w in enumerate((2, 4, 8, 16)):
        def bounds(m):
            q = np.arange(m)
            return np.clip(q - w // 2, 0, m), np.clip(q - w // 2 + w, 0, m)
        lr, hr = bounds(8)
        lc, hc = bounds(64)
        R = ((np.arange(8)[None] >= lr[:, None]) & (np.arange(8)[None] < hr[:, None])) * 1.0
        C = ((np.arange(64)[None] >= lc[:, None]) & (np.arange(64)[None] < hc[:, None])) * 1.0
        cnt = ((hr - lr)[:, None] * (hc - lc)[None, :]).astype(np.float64).reshape(512)
        K = np.kron(R, C) / cnt[:, None] - np.eye(512)
        box[g] = K.T
    box = box.reshape(4, 4, 128, 512).transpose(0, 2, 1, 3).reshape(4, 128, 2048)
    return k, sel.reshape(4, 512), oh, neg.astype(np.float32), np.ascontiguousarray(box)


COLS = [(f"{n}{l}", w) for l in range(2) for n, w in
        (("n1_", 8), ("nm_", 8), ("n2_", 8), ("cw_", 32), ("cb_", 8), ("qw_", 1), ("kw_", 1))] + [
    ("norm1", 8), ("norm2", 8), ("normf", 8), ("cw2", 48), ("psc", 4), ("c", 16), ("bmod", 48)]
ROWS = [(f"{n}{l}", w) for l in range(2) for n, w in
        (("gb_", 64), ("al_", 32), ("mn_", 256), ("sn_", 512), ("D_", 8), ("sl_", 64), ("lam_", 128))] + [
    ("al2", 8), ("dtb2", 8), ("dn", 128)]


def offsets(spec):
    out, at = {}, 0
    for n, w in spec:
        out[n] = (at, w)
        at += w
    return out, at


class Eng:

    def __init__(self, nc, h, name):
        self.h, self.q, self.n, self.seen = h, [], 0, {}
        self.sem = nc.alloc_semaphore("s_" + name)
        self.name = name

    def wait(self, *toks):
        for t in toks:
            if t is None:
                continue
            if isinstance(t, list):
                self.wait(*t)
                continue
            sem, v = t
            if self.seen.get(sem.name, 0) < v:
                self.seen[sem.name] = v
                self.q.append(lambda sem=sem, v=v: self.h.wait_ge(sem, v))

    def __call__(self, fn, *toks):
        self.wait(*toks)
        self.n += 1
        self.q.append(lambda: fn(self.h).then_inc(self.sem, 1))
        return (self.sem, self.n)

    def quiet(self, fn, *toks):
        self.wait(*toks)
        self.q.append(lambda: fn(self.h))

    def dma(self, fn, sem, *toks):
        self.wait(*toks)
        self.q.append(lambda: fn(self.h).then_inc(sem, 16))

    def now(self):
        return (self.sem, self.n) if self.n else None

    def run(self):
        for f in self.q:
            f()


class Bank:
    def __init__(self, ap, i, w, owner):
        self.ap, self.i, self.w, self.owner = ap, i, w, owner

    def free(self, *toks):
        self.owner.freed[self.i] = list(toks)
        self.owner.busy[self.i] = False


class Banks:

    def __init__(self, aps):
        self.aps, self.k = aps, -1
        self.freed = [[] for _ in aps]
        self.busy = [False] * len(aps)

    def take(self):
        for _ in self.aps:
            self.k = (self.k + 1) % len(self.aps)
            if not self.busy[self.k]:
                self.busy[self.k] = True
                return Bank(self.aps[self.k], self.k, self.freed[self.k], self)
        raise AssertionError("no bank")


def build(nc, A, out_x, dbg=None, upto=99):
    PE, V, S, G, SP = (Eng(nc, h, n) for h, n in (
        (nc.tensor, "pe"), (nc.vector, "dve"), (nc.scalar, "act"), (nc.gpsimd, "pool"), (nc.sync, "sp")))
    banks = Banks([nc.alloc_psum_tensor(f"ps{i}", [128, 512], F32) for i in range(8)])
    NM = 53000
    memu = nc.alloc_sbuf_tensor_at("memu", [128, 192], U32, offset=MEM_AT + 4 * NM)
    top = [0]

    where = {}

    def at(a, n, dt=F32):
        h = nc.alloc_sbuf_tensor_at(f"b{len(where)}", [128, n], dt, offset=MEM_AT + 4 * a)
        where[h.name] = a
        return h[:, :]

    def al(n):
        a = top[0]
        top[0] += (n + 7) // 8 * 8
        assert top[0] <= NM, (top[0], NM)
        return at(a, n)

    def fr(ap):
        return at(where[ap.tensor.name] + ap.offset, ap.shape[1], FR)

    def v3(ap, a):
        return ap.rearrange("p (a b) -> p a b", a=a)

    def v4(ap, a, b):
        return ap.rearrange("p (a b c) -> p a b c", a=a, b=b)

    ring = [al(SLOT) for _ in range(NSLOT)]
    ring_sem = [nc.alloc_semaphore(f"ring{i}") for i in range(NSLOT)]
    ring_n = [0] * NSLOT
    ring_free = [None] * NSLOT
    ring_k = [0]

    def grow(slots):
        ring_k[0] = len(ring)
        for r in slots:
            ring_sem.append(nc.alloc_semaphore(f"ring{len(ring)}"))
            ring.append(r)
            ring_n.append(0)
            ring_free.append(every())

    class Slot:
        pass

    def load(src, n=SLOT):
        i = ring_k[0] % len(ring)
        ring_k[0] += 1
        assert ring_free[i] != "busy", "slot"
        SP.dma(lambda h: h.dma_start(ring[i][:, 0:n], src), ring_sem[i], ring_free[i])
        ring_n[i] += 1
        ring_free[i] = "busy"
        s = Slot()
        s.ap, s.t, s.i = ring[i][:, 0:n], (ring_sem[i], 16 * ring_n[i]), i
        return s

    def done(s, *toks):
        ring_free[s.i] = list(toks)

    nsem = [0]
    dma_all = []

    def misc(E, dst, src, *toks, slow=False):
        sem = nc.alloc_semaphore(f"m{nsem[0]}")
        nsem[0] += 1
        E.dma(lambda h: h.dma_start(dst, src, allow_slow_non_contiguous=slow), sem, *toks)
        dma_all.append((sem, 16))
        return (sem, 16)

    def snap(name, ap, *toks):
        if dbg is not None:
            t = nc.dram_tensor("dbg_" + name, list(ap.shape), ap.dtype, kind="ExternalOutput")
            dbg.append("dbg_" + name)
            tk = misc(G, t.ap(), ap, *toks, V.now(), S.now(), PE.now())
            for e in (PE, V, S):
                e.wait(tk)

    def every():
        return [e.now() for e in (PE, V, S, G)] + dma_all[-40:]

    def barrier():
        t = every()
        for e in (PE, V, S, G):
            e.wait(*t)

    def mm(out, l, r, *w, start=True, stop=True, inc=False):
        f = lambda h: h.matmul(out, l, r, start=start, stop=stop)
        return PE(f, *w) if inc else PE.quiet(f, *w)

    def tr(out, i, *w, inc=False):
        k = i.shape[0]
        f = lambda h: h.transpose(out, i, ident[0:k, 0:k])
        return PE(f, *w) if inc else PE.quiet(f, *w)

    def tt(out, a, b, op, *w, E=None):
        return (E or V)(lambda h: h.tensor_tensor(out, a, b, op), *w)

    def ts(out, a, s1, op0, *w, s2=None, op1=None, E=None):
        if op1 is None:
            return (E or V)(lambda h: h.tensor_scalar(out, a, s1, None, op0), *w)
        return (E or V)(lambda h: h.tensor_scalar(out, a, s1, s2, op0, op1), *w)

    def stt(out, a, s, b, op0, op1, *w):
        return V(lambda h: h.scalar_tensor_tensor(out, a, s, b, op0, op1), *w)

    def cp(out, a, *w, E=None):
        if E is S:
            return S(lambda h: h.copy(out, a), *w)
        return (E or V)(lambda h: h.tensor_copy(out, a), *w)

    def act(out, a, f, *w, bias=0.0, scale=1.0, acc=None):
        if acc is not None:
            return S(lambda h: h.activation(out, a, f, bias=bias, scale=scale, accum_out=acc), *w)
        return S(lambda h: h.activation(out, a, f, bias=bias, scale=scale), *w)

    def rcp(out, a, *w):
        return V(lambda h: h.reciprocal(out, a), *w)

    class Unit:
        def __init__(self, hi, lo, i, w, owner):
            self.hi, self.lo, self.i, self.w, self.owner = hi, lo, i, w, owner

        def free(self, *t):
            self.owner.freed[self.i] = list(t)

    class Units:

        def __init__(self, region, n):
            self.n, self.k = n, -1
            self.hi = [fr(region[:, 2 * n * i:2 * n * i + n]) for i in range(region.shape[1] // (2 * n))]
            self.lo = [fr(region[:, 2 * n * i + n:2 * n * i + 2 * n]) for i in range(region.shape[1] // (2 * n))]
            self.freed = [[] for _ in self.hi]

        def take(self):
            self.k = (self.k + 1) % len(self.hi)
            return Unit(self.hi[self.k], self.lo[self.k], self.k, self.freed[self.k], self)

    def split(hi, lo, src, *w):
        t1 = cp(hi, src, *w, E=S)
        t2 = tt(lo, src, hi.bitcast(F32), ALU.subtract, t1)
        return [t1, t2]

    def mm3(out, l, r, *w, start, stop, inc):
        mm(out, l[0], r[0], *w, start=start, stop=False)
        mm(out, l[0], r[1], start=False, stop=False)
        return mm(out, l[1], r[0], start=False, stop=stop, inc=inc)

    kst = al(128 * len(CONSTS))
    K = {n: kst[:, i * 128:(i + 1) * 128] for i, n in enumerate(CONSTS)}
    ident = K["ident"]
    sel = al(512)
    coff, cn = offsets(COLS)
    roff, rn = offsets(ROWS)
    cols, rows = al(cn), al(rn)
    smw = al(512)
    poolw = al(512)
    t_c = [misc(S, kst, A["k_const"]), misc(S, sel[0:4, :], A["k_sel"]), misc(S, cols, A["cols"]),
           misc(S, rows, A["rows"]), misc(S, smw, A["smallw"]), misc(S, poolw, A["poolw"])]
    for e in (PE, V, S, G):
        e.wait(*t_c)
    swh, swl = fr(al(512)), fr(al(512))
    tsw = split(swh, swl, smw)
    PE.wait(*tsw)

    def col(n, i=0, w=1):
        return cols[:, coff[n][0] + i:coff[n][0] + i + w]

    def row(n):
        return rows[:, roff[n][0]:roff[n][0] + roff[n][1]]

    xT = v3(al(4096), 8)
    hTf = al(4096)
    hT = v3(hTf, 8)
    rstd = al(512)
    b4f = al(2048)
    bias4 = v3(b4f, 4)
    ctxS = v3(al(1024), 8)
    MOD = v3(al(96), 48)
    A1 = al(8)
    A2 = al(8)
    Ac = al(8)
    hs = al(128 * 4)
    base = top[0]
    print('base', base) if dbg is not None else None
    KD = [True]

    def reset():
        top[0] = base

    two = [al(512), al(512)]
    two_t = [None, None]
    nacc = rstd
    stat = {"acc": None}
    base = top[0]

    def stat_add(k, src, tok):
        n = src.shape[1]
        q = two[k % 2][:, 0:n]
        t = act(nacc[:, 0:n] if k == 0 else q, src, ACT.Square, tok, two_t[k % 2],
                stat["acc"] if k == 0 else None)
        if k:
            t = tt(nacc[:, 0:n], nacc[:, 0:n], q, ALU.add, t, stat["acc"])
            two_t[k % 2] = t
        stat["acc"] = t

    def norm_fm(src, dst, scale_col, n, shift_col=None, full=None, mid=None):
        b = banks.take()
        p = mm(b.ap[:, 0:n], K["one"], nacc[:, 0:n], stat["acc"], *b.w, inc=True)
        stat["acc"] = p
        r = rstd[:, 0:n]
        t = ts(r, b.ap[:, 0:n], 1.0 / D, ALU.mult, p, s2=EPS, op1=ALU.add)
        b.free(t)
        t = rcp(r, r, t)
        if mid is not None:
            mid()
        t = act(r, r, ACT.Sqrt, t)
        out = []
        held = None
        for k in range(9):
            if k < 8:
                tmp = two[k % 2][:, 0:n] if full is None else full[:, k, :]
                u = stt(tmp, src[:, k, :], scale_col(k), r, ALU.mult, ALU.mult, t, two_t[k % 2])
                if shift_col is not None:
                    u = ts(tmp, tmp, shift_col(k), ALU.add, u)
                hi, lo = dst(k)
                t1 = cp(hi, tmp, u, E=S)
            if held is not None:
                j, x, y, z, w = held
                w = [w, tt(x, y, z.bitcast(F32), ALU.subtract, w)]
                out.append(w)
                if full is None:
                    two_t[j % 2] = w
            held = (k, lo, tmp, hi, t1)
        return out

    def to_fm(src_tok, dst, nt, dep, stats=False):
        last = []
        for k in range(8):
            b = banks.take()
            for t in range(nt):
                p = tr(b.ap[:, t * 128:(t + 1) * 128], src_tok[:, t, k * 128:(k + 1) * 128], dep, *b.w, inc=(t == nt - 1))
            e = cp(dst[:, k, :], b.ap[:, 0:nt * 128], p, E=(S if k % 2 else None))
            b.free(e)
            last.append(e)
            if stats:
                stat_add(k, dst[:, k, :], e)
        return last

    def fm_parts(src, dst, dep):
        b = banks.take()
        for i in range(4):
            p = tr(b.ap[:, i * 128:(i + 1) * 128], src(i), dep, *b.w, inc=(i == 3))
        t = split(dst[0], dst[1], b.ap[:, :], p)
        b.free(*t)
        return t

    def silu(dst, src, tmp, *w):
        t = act(tmp, src, ACT.Tanh, *w, scale=0.5)
        t = ts(tmp, tmp, 0.5, ALU.mult, t, s2=0.5, op1=ALU.add)
        return tt(dst, src, tmp, ALU.mult, t)

    def softplus(dst, x, e, u, d, *w):
        t = act(d, x, ACT.Abs, *w)
        t = act(e, d, ACT.Exp, t, scale=-1.0)
        t = ts(u, e, 1.0, ALU.add, t)
        t2 = act(dst, u, ACT.Ln, t)
        t = ts(d, u, -1.0, ALU.add, t)
        t = tt(e, e, d, ALU.subtract, t)
        t = tt(dst, dst, e, ALU.add, t, t2)
        return stt(dst, x, 0.0, dst, ALU.max, ALU.add, t)

    def rms_tok(*a):
        for t in rms_steps(*a):
            pass
        return t

    def rms_steps(Y, G_, W, sq, ms, wrow, extra, *w):
        a = Y.shape[1]
        t = None
        for i in range(a):
            t = tt(sq[:, i], Y[:, i], Y[:, i], ALU.mult, *w)
            yield t
        t = V(lambda h: h.tensor_reduce(ms, sq, AX, ALU.add), t)
        t = ts(ms, ms, 1.0 / W, ALU.mult, t, s2=EPS, op1=ALU.add)
        t = rcp(ms, ms, t)
        t = act(ms, ms, ACT.Sqrt, t)
        yield t
        bc = ms.unsqueeze(3).to_broadcast([128, a, G_, W])
        for i in range(a):
            t1 = tt(Y[:, i], Y[:, i], bc[:, i], ALU.mult, t, *w)
            t1 = tt(Y[:, i], Y[:, i], wrow, ALU.mult, t1)
            if extra is not None:
                t1 = ts(Y[:, i], Y[:, i], extra, ALU.mult, t1) if isinstance(extra, float) else \
                    tt(Y[:, i], Y[:, i], extra[:, i], ALU.mult, t1)
            yield t1

    def transposes(src, dst, n, w, *dep):
        toks = []
        for j in range(0, n, 4):
            b = banks.take()
            m = min(4, n - j)
            for i in range(m):
                p = tr(b.ap[0:w, i * 128:(i + 1) * 128], src(j + i), *dep, *b.w, inc=(i == m - 1))
            e = cp(dst(j), v3(b.ap[0:w, 0:m * 128], m), p, E=(S if (j // 4) % 2 else None))
            b.free(e)
            toks.append(e)
        return toks

    hlo = [None]

    def parts(hi, lo, n=512):
        h, l = v3(fr(hi), 8), v3(fr(lo), 8)
        return lambda k: (h[:, k, 0:n], l[:, k, 0:n])

    def pipeline(items, ahead, side=None):
        for j in range(min(ahead, len(items))):
            items[j][0]()
        for i, (_, mm_, post) in enumerate(items):
            if i + ahead < len(items):
                items[i + ahead][0]()
            mm_()
            post()
            if side is not None:
                next(side, None)
        for _ in side or ():
            pass

    def early(items, n):
        for j in range(n):
            items[j][0]()
            items[j] = (lambda: None,) + tuple(items[j][1:])

    def ffn(idx, nm):
        reset()
        barrier()
        lo = al(4096)
        hp = parts(hTf, lo)
        GRP = (12, 10)
        ahi, alo = v3(fr(al(12 * 512)), 12), v3(fr(al(12 * 512)), 12)
        U = Units(al(8192), 1024)
        sl = {}
        th = []
        ready, st = {}, {"afree": None}
        items = []

        def up_item(f, fi, q):
            x = {}

            def split_():
                if f % 2 == 0:
                    sl[q] = [load(A["wg" if q == 0 else "wu"][idx, f // 2]), []]
                s, rel = sl[q]
                c = slice((f % 2) * 128, (f % 2) * 128 + 128)
                u = x["u"] = U.take()
                x["tw"] = split(v3(u.hi, 8), v3(u.lo, 8), v3(s.ap, 8)[:, :, c], s.t, *u.w)
                rel.append(x["tw"])
                if f % 2:
                    done(s, *rel)

            def mm_():
                u = x["u"]
                b = x["b"] = banks.take()
                for k in range(8):
                    t = mm3(b.ap[:, :], (v3(u.hi, 8)[:, k, :], v3(u.lo, 8)[:, k, :]), hp(k), x["tw"], th[k], *b.w,
                            start=(k == 0), stop=(k == 7), inc=(k == 7))
                u.free(t)
                st[q] = (b, t)

            def post():
                if q == 0:
                    return
                (bg, tg), (bu, tu) = st[0], st[1]
                e = two[f % 2]
                t = act(e, bg.ap[:, :], ACT.Tanh, tg, two_t[f % 2], scale=0.5)
                t = stt(e, e, 1.0, bg.ap[:, :], ALU.add, ALU.mult, t)
                bg.free(t)
                t = tt(e, e, bu.ap[:, :], ALU.mult, t, tu)
                bu.free(t)
                t = split(ahi[:, fi, :], alo[:, fi, :], e, t, st["afree"])
                two_t[f % 2] = t
                ready[fi] = t
            return split_, mm_, post

        def down_item(grp, nf, d, half):
            x = {}
            m = nf // 2

            def split_():
                if half == 0:
                    sl["d"] = [load(A["wd%d" % grp][idx, d], nf * 128), []]
                s, rel = sl["d"]
                u = x["u"] = U.take()
                x["hi"], x["lo"] = (v3(y[:, 0:m * 128], m) for y in (u.hi, u.lo))
                x["tw"] = split(x["hi"], x["lo"], v3(s.ap, nf)[:, half * m:half * m + m, :], s.t, *u.w)
                rel.append(x["tw"])
                if half:
                    done(s, *rel)

            def mm_():
                if half == 0:
                    st["b"] = banks.take()
                b = st["b"]
                for j in range(m):
                    n = half * m + j
                    t = mm3(b.ap[:, :], (x["hi"][:, j, :], x["lo"][:, j, :]), (ahi[:, n, :], alo[:, n, :]), x["tw"],
                            ready[n], *b.w, start=(n == 0), stop=(n == nf - 1), inc=(j == m - 1))
                x["u"].free(t)
                x["t"] = st["afree"] = t

            def post():
                if half == 0:
                    return
                b = st["b"]
                e = stt(xT[:, d, :], b.ap[:, :], 0.25, xT[:, d, :], ALU.mult, ALU.add, x["t"])
                b.free(e)
                if grp == 1:
                    stat_add(d, xT[:, d, :], e)
            return split_, mm_, post

        f0 = 0
        for grp, nf in enumerate(GRP):
            items += [up_item(f0 + fi, fi, q) for fi in range(nf) for q in range(2)]
            items += [down_item(grp, nf, d, half) for d in range(8) for half in range(2)]
            f0 += nf
        th += norm_fm(xT, hp, lambda k: col(nm, k), 512, mid=lambda: early(items, 2))
        pipeline(items, 2)

    def fm_items(src, nt, w, put, dep, U):
        sl = {}

        def item(i):
            x = {}

            def split_():
                if i == 0:
                    sl["s"] = [load(w), []]
                s, rel = sl["s"]
                u = x["u"] = U.take()
                x["tw"] = split(v3(u.hi, 8), v3(u.lo, 8), v3(s.ap, 8)[:, :, i * 128:(i + 1) * 128], s.t, *u.w)
                rel.append(x["tw"])
                if i:
                    done(s, *rel)

            def mm_():
                u = x["u"]
                hi, lo = v3(u.hi, 8), v3(u.lo, 8)
                b = x["b"] = banks.take()
                for k in range(8):
                    t = mm3(b.ap[:, 0:nt], (hi[:, k, :], lo[:, k, :]), src(k), x["tw"], dep[k], *b.w,
                            start=(k == 0), stop=(k == 7), inc=(k == 7))
                u.free(t)
                x["t"] = t

            def post():
                x["b"].free(put(i, x["b"].ap[:, 0:nt], x["t"]))
            return split_, mm_, post
        return [item(0), item(1)]

    def tok_items(src, nt, w, put, dep, U):
        sl = {}

        def item(half):
            x = {}

            def split_():
                if half == 0:
                    sl["s"] = [load(w), []]
                s, rel = sl["s"]
                u = x["u"] = U.take()
                x["tw"] = split(v3(u.hi, 4), v3(u.lo, 4), v3(s.ap, 8)[:, 4 * half:4 * half + 4, :], s.t, *u.w)
                rel.append(x["tw"])
                if half:
                    done(s, *rel)

            def mm_():
                if half == 0:
                    sl["b"] = [banks.take() for _ in range(nt)]
                u = x["u"]
                hi, lo = v3(u.hi, 4), v3(u.lo, 4)
                x["t"] = []
                for i in range(nt):
                    c = slice(i * 128, (i + 1) * 128)
                    b = sl["b"][i]
                    for j in range(4):
                        k = 4 * half + j
                        y = src(k)
                        t = mm3(b.ap[:, 0:256], (y[0][:, c], y[1][:, c]), (hi[:, j, :], lo[:, j, :]), x["tw"], dep[k],
                                *b.w, start=(k == 0), stop=(k == 7), inc=(j == 3))
                    x["t"].append(t)
                u.free(t)

            def post():
                if half:
                    for i in range(nt):
                        b = sl["b"][i]
                        b.free(put(i, b.ap[:, 0:256], x["t"][i]))
            return split_, mm_, post
        return [item(0), item(1)]

    def proj_small(src, nt, w, dst, dep):
        hi, lo = (v3(x[:, 128 * w:128 * w + 128], 8) for x in (swh, swl))
        b = banks.take()
        for i in range(nt):
            c = slice(i * 128, (i + 1) * 128)
            for k in range(8):
                x = src(k)
                t = mm3(b.ap[:, 16 * i:16 * i + 16], (x[0][:, c], x[1][:, c]), (hi[:, k, :], lo[:, k, :]), dep[k],
                        *b.w, start=(k == 0), stop=(k == 7), inc=(k == 7))
        e = cp(dst, v3(b.ap[:, 0:16 * nt], nt), t)
        b.free(e)
        return e

    def rel_table():
        reset()
        oh, rb, neg, F = al(640), al(4), al(640), v3(al(2560), 4)
        t = [misc(S, oh[0:32, :], A["k_oh"]), misc(S, rb[0:32, :], A["rel_bias"]), misc(S, neg, A["k_neg"])]
        es = []
        for h in range(4):
            l = rb[0:32, h:h + 1].to_broadcast([32, 128])
            for c0, n in ((0, 512), (512, 128)):
                b = banks.take()
                p = mm(b.ap[:, 0:n], l, oh[0:32, c0:c0 + n], *t, *b.w, inc=True)
                e = tt(F[:, h, c0:c0 + n], b.ap[:, 0:n], neg[:, c0:c0 + n], ALU.add, p, *t)
                b.free(e)
                es.append(e)
        Fd = nc.dram_tensor("F_scratch", [4, 128, 640], F32)
        t = misc(S, Fd.ap().rearrange("h p x -> p h x"), F, *es)
        src = bass.AP(tensor=Fd, offset=127, ap=[[639, 128], [128 * 640, 4], [1, 512]])
        return misc(S, bias4, src, t)

    def mixer(l):
        reset()
        barrier()
        lam_init = 0.8 - 0.6 * float(np.exp(-0.3 * l))
        G1 = v3(al(64), 4)
        SPx, e1, u1, d1, X = (v3(al(48), 4) for _ in range(5))
        Lc = v3(al(48), 4)
        TOT = v3(al(48), 4)
        Bg, cc, mt, em = (v3(al(16), 4) for _ in range(4))
        V1 = al(4 * 4 * 65).rearrange("p (t h c) -> p t h c", t=4, h=4)
        mo = v3(al(1024), 4)
        z = v3(al(2048), 4)
        dvt = v3(al(1024), 4)
        Yf = al(4096)
        Y = v3(Yf, 4)
        small = [al(64) for _ in range(12)]
        qkf = al(4096)
        qk, dqk = v3(qkf[:, 0:2048], 4), v3(qkf[:, 2048:4096], 4)
        xbc = v3(al(8 * 516), 8)
        tAB = al(4096)
        tA, tB, tC = tAB[:, 0:2048], tAB[:, 2048:4096], al(2048)
        crow, Mrow = tC[:, 1024:1536], tC[:, 1536:2048]
        cvt = [tC[:, 0:512], tC[:, 512:1024]]
        U = Units(tAB, 1024)
        hp = parts(hTf, Yf)
        th = []
        win = A["win"]
        items = []
        tq, tv, tz, tdv, tx, td = [], [], [], [], [], []

        def put_to(dst, w, out, E=None, view=None):
            def put(i, ps, t):
                out.append(cp(dst(i), view(ps) if view else ps, t, *w, E=E))
                return out[-1]
            return put

        conv_t = []
        held = []
        tzs = []

        def conv_tail():
            i, a, t = held.pop()
            conv_t.append(silu_tail(xbc[:, i, 3:515], a, xbc[:, i, 3:515], t))

        def put_xbc(blk):
            def put(i, ps, t):
                n = 2 * blk + i
                o = xbc[:, n, :]
                e = cp(o[:, 3:515], ps, t, tzero, E=S)
                a = cvt[n % 2]
                w = coff[f"cw_{l}"][0] + 4 * n
                t = ts(a, o[:, 0:512], cols[:, w:w + 1], ALU.mult, e, tzero, conv_t[-1] if conv_t else None,
                       s2=col(f"cb_{l}", n), op1=ALU.add)
                for j in range(1, 4):
                    t = stt(a, o[:, j:j + 512], cols[:, w + j:w + j + 1], a, ALU.mult, ALU.add, t)
                if held:
                    conv_tail()
                held.append((n, a, t))
                return e
            return put

        def silu_tail(dst, a, tmp, t):
            t = act(tmp, a, ACT.Tanh, t, scale=0.5)
            t = ts(tmp, tmp, 0.5, ALU.mult, t, s2=0.5, op1=ALU.add)
            return tt(dst, a, tmp, ALU.mult, t)

        tzero = V(lambda h: h.memset(xbc[:, :, 0:3], 0.0))
        ti_ = V(lambda h: h.memset(V1[:, :, :, 64:65], 1.0))
        items = []
        for blk in range(2):
            items += fm_items(hp, 512, win[l, blk], put_to(lambda i, blk=blk: qk[:, 2 * blk + i, :], [], tq, S), th, U)
        items += tok_items(hp, 4, win[l, 8], put_to(lambda i: V1[:, i, :, 0:64], [], tv, None, lambda ps: v3(ps, 4)),
                           th, U)
        xb = [fm_items(hp, 512, win[l, 2 + blk], put_xbc(blk), th, U) for blk in range(4)]
        tk = [tok_items(hp, 4, win[l, 10 + half],
                        put_to(lambda i, half=half: z[:, i, half * 256:half * 256 + 256], [], tz, S), th, U)
              for half in range(2)]
        tk.append(tok_items(hp, 4, win[l, 12], put_to(lambda i: dvt[:, i, :], [], tdv, S), th, U))
        tk.append(tok_items(hp, 4, win[l, 9], put_to(lambda i: mo[:, i, :], [], tv, S), th, U))
        for i in range(4):
            items += xb[i] + tk[i]
        for blk in range(2):
            items += fm_items(hp, 512, win[l, 6 + blk], put_to(lambda i, blk=blk: dqk[:, 2 * blk + i, :], [], td, S),
                              th, U)
        gt = {}

        def gates():
            yield
            tg = proj_small(hp, 4, l, G1, th)
            yield
            t = tt(G1, G1, v3(row(f"gb_{l}"), 4), ALU.add, tg)
            ta = ts(SPx[:, :, 0:4], G1[:, :, 4:8], -1.0, ALU.mult, t)
            tb = cp(SPx[:, :, 4:12], G1[:, :, 8:16], t)
            tsp = softplus(Lc, SPx, e1, u1, d1, ta, tb)
            td_ = cp(dts, Lc[:, :, 4:12], tsp)
            tA_ = act(small[1][:, 0:32], row(f"al_{l}"), ACT.Exp)
            t1 = ts(X[:, :, 0:4], Lc[:, :, 0:4], -1.0, ALU.mult, tsp)
            t2 = stt(X[:, :, 4:12], Lc[:, :, 4:12], -1.0, v3(small[1][:, 0:32], 4), ALU.mult, ALU.mult, tsp, tA_)
            yield
            yield
            b = banks.take()
            PE.wait(t1, t2, *b.w)
            mm(b.ap[:, 0:48], K["LE"], X.rearrange("p a b -> p (a b)"))
            mm(b.ap[:, 48:96], K["one"], X.rearrange("p a b -> p (a b)"))
            for i in range(4):
                for m in range(i + 1):
                    p = mm(b.ap[:, 96 + 4 * i:100 + 4 * i], K["LE"] if m == i else K["one"], X[:, m, 0:4],
                           start=(m == 0), stop=(m == i), inc=(i == 3 and m == 3))
            yield
            t1 = cp(Lc, v3(b.ap[:, 0:48], 4), p, td_, t1, t2)
            t2 = cp(TOT, v3(b.ap[:, 48:96], 4), p)
            t3 = cp(Bg, v3(b.ap[:, 96:112], 4), p)
            b.free(t3)
            gt["tLc"] = [t1, t2]
            tcc = tt(cc, G1[:, :, 0:4], Bg, ALU.subtract, t3)
            yield
            b = banks.take()
            PE.wait(tcc, *b.w)
            for i in range(4):
                p = tr(b.ap[0:4, i * 128:(i + 1) * 128], cc[:, i, :], inc=(i == 3))
            t = cp(crow[0:4, :], b.ap[0:4, :], p)
            b.free(t)
            tm = V(lambda h: h.tensor_tensor_scan(Mrow[0:4, :], crow[0:4, :], crow[0:4, :], 0.0, ALU.max, ALU.max), t)
            yield
            b = banks.take()
            PE.wait(tm, *b.w)
            for i in range(4):
                p = tr(b.ap[:, 4 * i:4 * i + 4], Mrow[0:4, i * 128:(i + 1) * 128], inc=(i == 3))
            t = tt(mt, Bg, v3(b.ap[:, 0:16], 4), ALU.add, p)
            b.free(t)
            gt["tem"] = act(em, mt, ACT.Exp, t, scale=-1.0)
            lam, lr = small[6], row(f"lam_{l}")
            pr = small[10]
            t = tt(pr[:, 0:32], lr[:, 0:32], lr[:, 32:64], ALU.mult)
            t = tt(pr[:, 32:64], lr[:, 64:96], lr[:, 96:128], ALU.mult, t)
            t = V(lambda h: h.tensor_reduce(lam[:, 0:2], v3(pr, 2), AX, ALU.add), t)
            t = act(lam[:, 2:4], lam[:, 0:2], ACT.Exp, t)
            t = tt(lam[:, 4:5], lam[:, 2:3], lam[:, 3:4], ALU.subtract, t)
            gt["lam"] = ts(lam[:, 5:6], lam[:, 4:5], lam_init, ALU.add, t)
            while len(tz) < 8:
                yield
            for i in range(4):
                two_t[i % 2] = silu(z[:, i, :], z[:, i, :], two[i % 2], *tz, two_t[i % 2])
                tzs.append(two_t[i % 2])
                yield
            while len(tv) < 8:
                yield
            mof = mo.rearrange("p a b -> p (a b)")
            t = act(mof, mof, ACT.Tanh, *tv, scale=0.5)
            tv.append(ts(mof, mof, 0.5, ALU.mult, t, s2=0.5, op1=ALU.add))

        dts = v3(small[0][:, 0:32], 4)
        th += norm_fm(xT, hp, lambda k: col(f"nm_{l}", k), 512, mid=lambda: early(items, 1))
        pipeline(items, 1, gates())
        conv_tail()
        tem, t1 = gt["tem"], gt["tLc"][1]
        snap(f"X{l}", X)
        snap(f"Mrow{l}", Mrow[0:4, :])
        XS, XD = v3(hTf[:, 0:2048], 4), v3(hTf[:, 2048:4096], 4)
        txs = transposes(lambda n: xbc[:, n // 4, 3 + (n % 4) * 128:3 + (n % 4) * 128 + 128],
                         lambda n: XS[:, :, (n // 4) * 128:(n // 4) * 128 + 128], 16, 128, *conv_t)
        snap(f"XS{l}", XS)
        txd = None
        for i in range(4):
            txd = tt(XD[:, i, :].rearrange("p (h c) -> p h c", h=8), XS[:, i, :].rearrange("p (h c) -> p h c", h=8),
                     dts[:, i, :].unsqueeze(2).to_broadcast([128, 8, 64]), ALU.mult, *txs)

        Sd = [v3(tA, 4), v3(tB, 4)]
        E = [tC[:, 0:512], tC[:, 512:1024]]
        dg = [tC[:, 1024:1152], tC[:, 1152:1280]]
        Er, dgr, Sdr = [None, None], [None, None], [None, None]
        PE.wait(*tq, *tv, ti_)
        cnt = 0
        tY = []
        def heads_a(h):
            nonlocal cnt
            bm = banks.take()
            pm = mm(bm.ap[:, :], sel[0:4, h * 128:(h + 1) * 128], Mrow[0:4, :], *bm.w, inc=True)
            r0 = (h % 2) * 64
            qh, kh = qk[r0:r0 + 64, h // 2, :], qk[r0:r0 + 64, 2 + h // 2, :]
            sd = Sd[h % 2]
            got = []
            for si in range(4):
                s0 = si * 128
                x = cnt % 2
                cnt += 1
                t = tt(dg[x], bm.ap[:, s0:s0 + 128], K["NEGU"], ALU.add, pm, dgr[x])
                t1 = act(E[x][:, s0:s0 + 128], dg[x], ACT.Exp, t, Er[x], bias=cc[:, si, h:h + 1], scale=-1.0)
                dgr[x] = t1
                if si < 3:
                    t1 = act(E[x][:, s0 + 128:512], bm.ap[:, s0 + 128:512], ACT.Exp, pm, Er[x],
                             bias=cc[:, si, h:h + 1], scale=-1.0)
                b = banks.take()
                p = mm(b.ap[:, s0:512], kh[:, s0:s0 + 128], qh[:, s0:512], *b.w, inc=True)
                t = stt(sd[:, si, s0:512], b.ap[:, s0:512], 0.125, E[x][:, s0:512], ALU.mult, ALU.mult,
                        p, t1, Sdr[h % 2])
                b.free(t)
                Er[x] = t
                got.append(t)
            bm.free(t1, got[-1])
            return got

        def heads_b(h, got):
            sd = Sd[h % 2]
            b = banks.take()
            PE.wait(*b.w)
            for ti in range(4):
                for si in range(ti + 1):
                    p = mm(b.ap[:, ti * 65:ti * 65 + 65], sd[:, si, ti * 128:(ti + 1) * 128], V1[:, si, h, :],
                           got[si], start=(si == 0), stop=(si == ti), inc=(si == ti))
            Sdr[h % 2] = p
            return b, p

        def heads_c(h, b, p):
            o = v3(b.ap[:, 0:260], 4)
            den = small[2 + h % 2][:, 0:4].unsqueeze(2)
            t = act(den, o[:, :, 64:65], ACT.Abs, p, *(tY[-2:-1]))
            t = tt(den, den, em[:, :, h:h + 1], ALU.max, t, tem)
            t = rcp(den, den, t)
            t = tt(Y[:, :, h * 64:h * 64 + 64], o[:, :, 0:64], den.to_broadcast([128, 4, 64]), ALU.mult, t)
            b.free(t)
            tY.append(t)

        tn = []

        def dqk_norm(i):
            s = act(two[0], dqk[:, i, :], ACT.Square, *td, two_t[0])
            b = banks.take()
            p = mm(b.ap[:, :], K["b32"], two[0], s, *b.w, inc=True)
            t = ts(two[1], b.ap[:, :], EPS, ALU.add, p, two_t[1])
            b.free(t)
            t = rcp(two[1], two[1], t)
            t = act(two[1], two[1], ACT.Sqrt, t)
            t = stt(dqk[:, i, :], dqk[:, i, :], col(f"qw_{l}" if i < 2 else f"kw_{l}"), two[1], ALU.mult, ALU.mult, t)
            two_t[0], two_t[1] = p, t
            tn.append(t)

        Sdr = [txd, txd]
        ga = heads_a(0)
        for h in range(4):
            gn = heads_a(h + 1) if h < 3 else None
            b, p = heads_b(h, ga)
            heads_c(h, b, p)
            dqk_norm(h)
            ga = gn
        snap(f"dqk{l}", dqk)
        snap(f"hm{l}", Y[:, :, 0:256])
        Ym = Y[:, :, 0:256].rearrange("p a (g w) -> p a g w", g=4)
        tym = rms_steps(Ym, 4, 64, v4(tC[:, 0:1024], 4, 4), v3(small[4][:, 0:16], 4),
                        v3(row(f"mn_{l}"), 4), mo.rearrange("p a (g w) -> p a g w", g=4), *tv, *tY)

        bia = al(16 * 8)
        bi = {}
        tb_ = None
        for si in range(4):
            for ti in range(si, 4):
                a = bia[:, (si * 4 + ti) * 8:(si * 4 + ti) * 8 + 8]
                bi[si, ti] = a
                if ti == si:
                    tb_ = ts(a, Lc[:, si, 4:12], -1.0, ALU.mult, *gt["tLc"])
                else:
                    tb_ = tt(a, bi[si, ti - 1], TOT[:, ti - 1, 4:12], ALU.add, tb_)
        CB = v3(xbc.rearrange("p a b -> p (a b)")[:, 0:2048], 4)
        Es = [v3(tB, 4), v3(tA, 4)]
        dg2 = [tC[:, 1024:1536], tC[:, 1536:2048]]
        tEr, tdg = [[PE.now(), V.now(), *txs]] * 2, [None, None]
        tEr = list(tEr)
        tCB, pv_last = None, None
        def ssd_a(h):
            nonlocal tCB
            g = h // 4
            if h % 4 == 0:
                tCB = []
                for si in range(4):
                    s0 = si * 128
                    b = banks.take()
                    p = mm(b.ap[:, s0:512], xbc[:, 4 + g, 3 + s0:3 + s0 + 128], xbc[:, 6 + g, 3 + s0:515],
                           *conv_t, *b.w, inc=True)
                    e = cp(CB[:, si, s0:512], b.ap[:, s0:512], p, V.now(), E=(S if si % 2 else None))
                    b.free(e)
                    tCB.append(e)
            bl = banks.take()
            PE.wait(*bl.w)
            for i in range(4):
                pl = mm(bl.ap[:, i * 128:(i + 1) * 128], X[:, i, 4 + h:5 + h].to_broadcast([128, 128]), K["LE"],
                        inc=(i == 3))
            x = h % 2
            Eh = Es[x]
            t = tt(v3(dg2[x], 4), v3(bl.ap[:, :], 4), K["NEGU"].unsqueeze(1).to_broadcast([128, 4, 128]),
                   ALU.subtract, pl, tdg[x])
            tl = t
            got = []
            for si in range(4):
                s0 = si * 128
                t1 = act(Eh[:, si, s0:s0 + 128], dg2[x][:, s0:s0 + 128], ACT.Exp, tl, tEr[x], tb_,
                         bias=bi[si, si][:, h:h + 1])
                tdg[x] = t1
                for ti in range(si + 1, 4):
                    t1 = act(Eh[:, si, ti * 128:ti * 128 + 128], bl.ap[:, ti * 128:ti * 128 + 128], ACT.Exp, pl,
                             bias=bi[si, ti][:, h:h + 1])
                got.append(tt(Eh[:, si, s0:512], Eh[:, si, s0:512], CB[:, si, s0:512], ALU.mult, t1, *tCB))
            bl.free(t1, tl)
            return got

        def ssd_b(h, got):
            x = h % 2
            Eh = Es[x]
            b = banks.take()
            PE.wait(*b.w, txd)
            for ti in range(4):
                for si in range(ti + 1):
                    p = mm(b.ap[:, ti * 64:ti * 64 + 64], Eh[:, si, ti * 128:(ti + 1) * 128],
                           XD[:, si, h * 64:h * 64 + 64], got[si], start=(si == 0), stop=(si == ti), inc=(si == ti))
            tEr[x] = p
            t = stt(Y[:, :, 256 + h * 64:320 + h * 64], XS[:, :, h * 64:h * 64 + 64], row(f"D_{l}")[:, h:h + 1],
                    v3(b.ap[:, 0:256], 4), ALU.mult, ALU.add, p)
            b.free(t)
            yh = Y[:, :, 256 + h * 64:320 + h * 64]
            return tt(yh, yh, z[:, :, h * 64:h * 64 + 64], ALU.mult, t, *tzs)

        ga = ssd_a(0)
        for h in range(8):
            gn = ssd_a(h + 1) if h < 7 else None
            t = ssd_b(h, ga)
            ga = gn
            for _ in range(2):
                next(tym, None)
        for _ in tym:
            pass
        snap(f"ym{l}", Y[:, :, 0:256])
        snap(f"ssd{l}", Y[:, :, 256:768])

        def ssm_norm(ty):
            ms = small[5][:, 0:8]
            w = row(f"sn_{l}")
            Yg = lambda i, g: Y[:, i, 256 + g * 256:512 + g * 256]
            for i in range(4):
                for g in range(2):
                    q = tC[:, (2 * i + g) * 256:(2 * i + g) * 256 + 256]
                    t = act(q, Yg(i, g), ACT.Square, ty, acc=ms[:, 2 * i + g:2 * i + g + 1])
                yield
            t = ts(ms, ms, 1.0 / 256, ALU.mult, t, s2=EPS, op1=ALU.add)
            t = rcp(ms, ms, t)
            t = act(ms, ms, ACT.Sqrt, t)
            yield
            for i in range(4):
                for g in range(2):
                    stt(Yg(i, g), Yg(i, g), ms[:, 2 * i + g:2 * i + g + 1], w[:, g * 256:g * 256 + 256], ALU.mult,
                        ALU.mult, t)
                yield

        V.wait(PE.now(), S.now())
        S.wait(PE.now(), V.now())
        sn = ssm_norm(t)
        lam, tlam = small[6], gt["lam"]
        Lg = [[tA[:, (2 * i + j) * 512:(2 * i + j) * 512 + 512] for j in range(2)] for i in range(2)]
        Aw = [tB[:, i * 512:i * 512 + 512] for i in range(2)]
        AT = [tB[:, 1024 + i * 512:1536 + i * 512] for i in range(2)]
        st = small[8:10]
        tLr, tAr, tATr = [None, None], [None, None], [None, None]
        PE.wait(*tn, *tdv)
        cnt = 0
        tyd = None
        def diff_a(n_):
            h, ti = n_ // 4, n_ % 4
            x = n_ % 2
            n = (ti + 1) * 128
            ex = []
            m = st[x]
            tl = []
            for c in range(2):
                r0 = (h % 2) * 64 + c * 32
                b = banks.take()
                p = mm(b.ap[:, 0:n], dqk[r0:r0 + 32, h // 2, ti * 128:n], dqk[r0:r0 + 32, 2 + h // 2, 0:n],
                       *b.w, inc=True)
                L = Lg[x][c]
                t = stt(L[:, 0:n], b.ap[:, 0:n], 32.0 ** -0.5, bias4[:, h, 512 - n:512], ALU.mult, ALU.add,
                        p, tLr[x])
                b.free(t)
                tl.append(t)
            for c in range(2):
                tl[c] = V(lambda h_, L=Lg[x][c], c=c: h_.reduce_max(m[:, c:c + 1], L[:, 0:n], AX), tl[c])
            t = ts(m[:, 2:4], m[:, 0:2], -1.0, ALU.mult, *tl)
            for c in range(2):
                L = Lg[x][c]
                ex.append(act(L[:, 0:n], L[:, 0:n], ACT.Exp, t, bias=m[:, 2 + c:3 + c], acc=m[:, 4 + c:5 + c]))
            return ex

        def diff_b(n_, ex):
            h, ti = n_ // 4, n_ % 4
            x = n_ % 2
            n = (ti + 1) * 128
            m = st[x]
            t = rcp(m[:, 6:8], m[:, 4:6], *ex)
            t = tt(m[:, 8:9], m[:, 7:8], lam[:, 5:6], ALU.mult, t, tlam)
            t = ts(Lg[x][1][:, 0:n], Lg[x][1][:, 0:n], m[:, 8:9], ALU.mult, t)
            t = stt(Aw[x][:, 0:n], Lg[x][0][:, 0:n], m[:, 6:7], Lg[x][1][:, 0:n], ALU.mult, ALU.subtract, t, tAr[x])
            tLr[x] = t
            b = banks.take()
            for si in range(ti + 1):
                p = tr(b.ap[:, si * 128:si * 128 + 128], Aw[x][:, si * 128:si * 128 + 128], t, *b.w, inc=(si == ti))
            tAr[x] = p
            t = cp(AT[x][:, 0:n], b.ap[:, 0:n], p, tATr[x], E=S)
            b.free(t)
            return t

        def diff_c(n_, t):
            h, ti = n_ // 4, n_ % 4
            x = n_ % 2
            b = banks.take()
            for si in range(ti + 1):
                p = mm(b.ap[:, 0:64], AT[x][:, si * 128:si * 128 + 128], dvt[:, si, h * 64:h * 64 + 64], t, *b.w,
                       start=(si == 0), stop=(si == ti), inc=(si == ti))
            tATr[x] = p
            t = cp(Y[:, ti, 768 + h * 64:832 + h * 64], b.ap[:, 0:64], p, E=S)
            b.free(t)
            return t

        A_, B_ = {0: diff_a(0)}, {}
        for n_ in range(17):
            if n_ + 1 < 16:
                A_[n_ + 1] = diff_a(n_ + 1)
            if n_ < 16:
                B_[n_] = diff_b(n_, A_[n_])
            if n_ >= 1:
                tyd = diff_c(n_ - 1, B_[n_ - 1])
            next(sn, None)
        for _ in sn:
            pass
        snap(f"ys{l}", Y[:, :, 256:768])
        snap(f"od{l}", Y[:, :, 768:1024])
        Yd = Y[:, :, 768:1024].rearrange("p a (g w) -> p a g w", g=4)
        tyd = rms_tok(Yd, 4, 64, v4(tC[:, 0:1024], 4, 4), v3(small[7][:, 0:16], 4),
                      row(f"sl_{l}").unsqueeze(1).to_broadcast([128, 4, 64]), 1.0 - lam_init, tyd)
        snap(f"Y{l}", Y)
        dst = parts(hTf, qkf)
        U = Units(tAB, 1024)
        S.wait(PE.now(), V.now())
        V.wait(PE.now())
        out_w(A["wout"], l, None, dst, lambda: [fm_parts(lambda i, k=k: Y[:, i, k * 128:(k + 1) * 128], dst(k), tyd)
                                                for k in range(8)], U)

    def out_w(wout, l, gain, src, make, U):
        items, dep = [], []
        for blk in range(4):
            def put(i, ps, t, blk=blk):
                k = 2 * blk + i
                if gain is None:
                    e = tt(xT[:, k, :], ps, xT[:, k, :], ALU.add, t)
                else:
                    e = stt(xT[:, k, :], ps, gain(k), xT[:, k, :], ALU.mult, ALU.add, t)
                stat_add(k, xT[:, k, :], e)
                return e
            items += fm_items(src, 512, wout[l, blk], put, dep, U)
        early(items, 1)
        dep += make()
        pipeline(items, len(U.hi) // 2)

    def modulation():
        reset()
        barrier()
        cs, tmp = v3(al(16), 8), al(16)
        t = silu(cs.rearrange("p a b -> p (a b)"), col("c", 0, 16), tmp)
        MR = [al(512), al(512)]
        r = [None, None]
        bt = banks.take()
        PE.wait(t, *bt.w)
        for j in range(12):
            b = banks.take()
            for half in range(2):
                s = load(A["wmod"][j * 2 + half])
                w4 = v3(s.ap, 4)
                for k in range(4):
                    kk = half * 4 + k
                    p = mm(b.ap[0:2, :], cs[:, kk, :], w4[:, k, :], s.t, *b.w, start=(kk == 0), stop=(kk == 7),
                           inc=(k == 3))
                done(s, p)
            e = cp(MR[j % 2][0:2, :], b.ap[0:2, :], p, r[j % 2], E=(S if j % 2 else None))
            b.free(e)
            for i in range(4):
                q = 4 * j + i
                r[j % 2] = tr(bt.ap[:, 2 * q:2 * q + 2], MR[j % 2][0:2, i * 128:(i + 1) * 128], e, inc=(i == 3))
        t = tt(MOD, v3(bt.ap[:, 0:96], 48), col("bmod", 0, 48).unsqueeze(2).to_broadcast([128, 48, 2]), ALU.add,
               r[1], r[0])
        bt.free(t)
        stt(A1.unsqueeze(2), MOD[:, 8:16, 0:1], 1.0, col("norm1", 0, 8).unsqueeze(2), ALU.add, ALU.mult, t)
        stt(A2.unsqueeze(2), MOD[:, 32:40, 0:1], 1.0, col("norm2", 0, 8).unsqueeze(2), ALU.add, ALU.mult, t)
        stt(Ac.unsqueeze(2), MOD[:, 8:16, 1:2], 1.0, col("norm1", 0, 8).unsqueeze(2), ALU.add, ALU.mult, t)
        snap("MOD", MOD)

    def convs(raw, n, tmp, tile0, dst, scale, tzero):
        todo, conv, fin, pend = [], {}, {}, []
        nr = raw.shape[1]

        def put(i, ps, t):
            e = cp(raw[:, i % nr, 2:n + 2], ps, t, tzero, conv[i - nr] if i >= nr else None, E=S)
            todo.append((i, e))
            return e

        def finish():
            i, sq, x, t = pend.pop()
            b = banks.take()
            p = mm(b.ap[:, 0:n], K["one"], sq, t, *b.w, inc=True)
            t = ts(x, b.ap[:, 0:n], EPS, ALU.add, p)
            b.free(t)
            t = rcp(x, x, t)
            t = act(x, x, ACT.Sqrt, t)
            fin[i] = stt(dst(i), dst(i), scale(i), x, ALU.mult, ALU.mult, t)

        def gen():
            while True:
                if pend:
                    finish()
                if todo:
                    i, e = todo.pop(0)
                    r = raw[:, i % nr, :]
                    x, y = tmp[i % 2], tmp[2 + i % 2]
                    w = coff["cw2"][0] + 4 * (tile0 + i)
                    t = ts(x, r[:, 0:n], cols[:, w:w + 1], ALU.mult, e)
                    for j in range(1, 4):
                        t = stt(x, r[:, j:j + n], cols[:, w + j:w + j + 1], x, ALU.mult, ALU.add, t)
                    conv[i] = t
                    t = silu(dst(i), x, y, t)
                    if scale(i) is None:
                        fin[i] = t
                    else:
                        pend.append((i, x, y, act(x, dst(i), ACT.Square, t)))
                yield
        return put, gen(), fin

    def delta(nt, kT, Kt, Vt, qT, ab, tab, Sst, O, dep):
        w8 = lambda: v3(al(8 * nt), nt)
        a, beta, x = w8(), w8(), w8()
        e, u, d = w8(), w8(), w8()
        nb, eg, bg, tail, etot = w8(), w8(), w8(), w8(), w8()
        for i in range(nt):
            t = tt(a[:, i, :], ab[:, i, 0:8], row("dtb2"), ALU.add, tab)
        t = softplus(x, a, e, u, d, t)
        t2 = act(d[:, 0, :], row("al2"), ACT.Exp, t)
        for i in range(nt):
            tx = stt(x[:, i, :], x[:, i, :], -1.0, d[:, 0, :], ALU.mult, ALU.mult, t, t2)
        bb = ab[:, :, 8:16]
        t = act(e, bb, ACT.Abs, tx, tab)
        t = act(e, e, ACT.Exp, t, scale=-1.0)
        t = ts(e, e, 1.0, ALU.add, t)
        t = rcp(e, e, t)
        t2 = ts(beta, bb, 0.0, ALU.min, t)
        t2 = act(beta, beta, ACT.Exp, t2)
        t = tt(beta, beta, e, ALU.mult, t2)
        tnb = ts(nb, beta, -1.0, ALU.mult, t)
        b = banks.take()
        PE.wait(tx, *b.w)
        n8 = 8 * nt
        for i in range(nt):
            for dr in range(2):
                c = slice(8 * i + 4 * dr, 8 * i + 4 * dr + 4)
                xs = x[:, i, 4 * dr:4 * dr + 4]
                mm(b.ap[:, c], K["LE" if dr == 0 else "GE"], xs)
                mm(b.ap[:, n8 + c.start:n8 + c.stop], K["GT" if dr == 0 else "LT"], xs)
        p = mm(b.ap[:, 2 * n8:3 * n8], K["one"], x.rearrange("p a b -> p (a b)"), inc=True)
        t1 = act(eg, v3(b.ap[:, 0:n8], nt), ACT.Exp, p)
        t2 = act(tail, v3(b.ap[:, n8:2 * n8], nt), ACT.Exp, p)
        t3 = act(etot, v3(b.ap[:, 2 * n8:3 * n8], nt), ACT.Exp, p)
        b.free(t3)
        tbg = tt(bg, beta, eg, ALU.mult, t1, tnb)
        snap(f"x2_{nt}", x)
        part = lambda m, o: [m[:, o + 128 * q:o + 128 * q + 128] for q in range(8)]
        XB, kbg, vb, kt = (part(hTf, 1024 * q) for q in range(4))
        P_, Tb = part(b4f, 0), part(b4f, 1024)
        Ex = [al(256) for _ in range(8)]
        wT, uu = part(al(1024), 0), part(al(1024), 0)
        W = part(al(1024), 0) if qT is not None else None
        LB = [al(384) for _ in range(8)]
        Yb = [al(64) for _ in range(8)]
        barrier()
        J = range(8)
        for step in range(nt):
            tile = [step if j < 4 else nt - 1 - step for j in J]
            sc = lambda m, j: m[:, tile[j], j:j + 1]
            cs = lambda j: slice(tile[j] * 128, tile[j] * 128 + 128)
            hh = lambda j: j % 4
            tE, tPb, tP, tkb, tvb, tkt, tW = ({} for _ in range(7))
            for j in J:
                f = j < 4
                t = ts(XB[j], K["GT"] if f else K["LT"], sc(x, j), ALU.mult, PE.now() if j == 0 else None)
                b = banks.take()
                mm(b.ap[:, 0:128], K["LE"] if f else K["GE"], XB[j], t, *b.w)
                p = mm(b.ap[:, 128:256], XB[j], K["LE"] if f else K["GE"], inc=True)
                t = act(Ex[j], b.ap[:, 0:256], ACT.Exp, p, V.now(), G.now())
                b.free(t)
                m0 = CO["GT"] if f else CO["LT"]
                tE[j] = G(lambda h, j=j, m0=m0: h.tensor_tensor(Ex[j], Ex[j], kst[:, m0:m0 + 256], ALU.mult), t)
            for j in J:
                kh = kT[:, hh(j), cs(j)]
                b = banks.take()
                p = mm(b.ap[:, 0:128], kh, kh, *b.w, inc=True)
                if qT is not None:
                    p = mm(b.ap[:, 128:256], kh, qT[:, hh(j), cs(j)], inc=True)
                tP[j] = t = stt(P_[j], b.ap[:, 0:128], sc(nb, j), Ex[j][:, 0:128], ALU.mult, ALU.mult, p, tE[j])
                if qT is not None:
                    t = tt(W[j], b.ap[:, 128:256], Ex[j][:, 128:256], ALU.mult)
                    tW[j] = t
                b.free(t)
                tPb[j] = tt(LB[j][:, 0:128], P_[j], K["bd"], ALU.mult, tP[j], E=G)
                kt_, vt_ = Kt[:, tile[j], hh(j) * 128:hh(j) * 128 + 128], Vt[:, tile[j], hh(j) * 128:hh(j) * 128 + 128]
                tkb[j] = act(kbg[j], kt_, ACT.Copy, scale=sc(bg, j))
                tvb[j] = ts(vb[j], vt_, sc(beta, j), ALU.mult)
                tkt[j] = act(kt[j], kt_, ACT.Copy, scale=sc(tail, j))
            tL, tT = {}, {}
            for j in J:
                b = banks.take()
                p = tr(b.ap[:, 0:128], LB[j][:, 0:128], tPb[j], *b.w, inc=True)
                tL[j] = cp(LB[j][:, 128:256], b.ap[:, 0:128], p, E=S)
                tT[j] = tt(LB[j][:, 256:384], b.ap[:, 0:128], ident, ALU.add, p, tL[j])
                b.free(tL[j], tT[j])
            for lev in range(6):
                for j in J:
                    b = banks.take()
                    L = LB[j]
                    if lev == 5:
                        p = mm(b.ap[:, 256:384], L[:, 0:128], L[:, 256:384], tL[j], tT[j], *b.w, inc=True)
                    else:
                        hi = 256 if lev == 0 else 384
                        mm(b.ap[:, 128:hi], L[:, 0:128], L[:, 128:hi], tL[j], tT[j], *b.w)
                        p = mm(b.ap[:, 0:128], L[:, 128:256], L[:, 0:128], inc=True)
                        tL[j] = cp(L[:, 0:256], b.ap[:, 0:256], p, E=S)
                    if lev:
                        tT[j] = tt(L[:, 256:384], b.ap[:, 256:384], L[:, 256:384], ALU.add, p, tL[j])
                    b.free(tL[j], tT[j])
            t2 = {}
            for j in J:
                TT = LB[j][:, 256:384]
                b = banks.take()
                tr(b.ap[:, 0:128], TT, tT[j], *b.w)
                lo, hi = (0, 64) if j < 4 else (64, 0)
                p = mm(b.ap[lo:lo + 64, 128:192], P_[j][hi:hi + 64, lo:lo + 64], TT[hi:hi + 64, hi:hi + 64], tP[j], inc=True)
                t1 = cp(Tb[j], b.ap[:, 0:128], p, E=S)
                t3 = cp(Yb[j][lo:lo + 64, :], b.ap[lo:lo + 64, 128:192], p, E=S)
                b.free(t1, t3)
                t2[j] = t3
            for j in J:
                TT = LB[j][:, 256:384]
                lo, hi = (0, 64) if j < 4 else (64, 0)
                b = banks.take()
                p = mm(b.ap[lo:lo + 64, 0:64], Tb[j][lo:lo + 64, lo:lo + 64], Yb[j][lo:lo + 64, :], t2[j], *b.w, inc=True)
                tT[j] = cp(TT[lo:lo + 64, hi:hi + 64], b.ap[lo:lo + 64, 0:64], p)
                b.free(tT[j])
            tu = {}
            for j in J:
                TT = LB[j][:, 256:384]
                b = banks.take()
                mm(b.ap[:, 0:128], kbg[j], TT, tT[j], tkb[j], tvb[j], *b.w)
                p = mm(b.ap[:, 128:256], TT, vb[j], inc=True)
                t1 = cp(wT[j], b.ap[:, 0:128], p, E=S)
                t3 = cp(uu[j], b.ap[:, 128:256], p, t1)
                b.free(t1, t3)
                tu[j] = [t1, t3]
            if step == 0:
                snap(f"LB_{nt}", LB[0])
                snap(f"LB4_{nt}", LB[4])
            tun, bq = {}, {}
            for j in J:
                b = banks.take()
                p = mm(b.ap[:, 0:128], wT[j], Sst[:, j, :], *tu[j], *b.w, dep, inc=True)
                tun[j] = stt(uu[j], b.ap[:, 0:128], -1.0, uu[j], ALU.mult, ALU.add, p)
                b.free(tun[j])
            for j in J:
                b = banks.take()
                PE.wait(*b.w, tun[j], tkt[j])
                p = mm(b.ap[:, 0:128], kt[j], uu[j], inc=(qT is None))
                if qT is not None:
                    mm(b.ap[:, 128:256], qT[:, hh(j), cs(j)], Sst[:, j, :])
                    p = mm(b.ap[:, 256:384], W[j], uu[j], tW[j], inc=True)
                t = stt(Sst[:, j, :], Sst[:, j, :], sc(etot, j), b.ap[:, 0:128], ALU.mult, ALU.add, p)
                dep = t
                if qT is not None:
                    o = O[:, tile[j], hh(j) * 128:hh(j) * 128 + 128]
                    t = stt(o, b.ap[:, 128:256], sc(eg, j), o, ALU.mult, ALU.add, p)
                    t = tt(o, b.ap[:, 256:384], o, ALU.add, t)
                b.free(t)

    CO = {n: i * 128 for i, n in enumerate(CONSTS)}

    def steps(side, fin, n):
        while len(fin) < n:
            next(side)
            yield

    def context():
        reset()
        barrier()
        kT = v3(al(4 * 256), 4)
        Kt, Vt = v3(al(1024), 2), v3(al(1024), 2)
        ab = v3(al(32), 2)
        mark = top[0]
        cT = v3(al(8 * 256), 8)
        ct = v3(al(2048), 2)
        t = misc(S, ct, A["ctx"].rearrange("(t p) d -> p t d", p=128))
        to_fm(ct, cT, 2, t, stats=True)
        hp = parts(hTf, al(4096), 256)
        U = Units(al(8192), 1024)
        th = norm_fm(cT, hp, lambda k: Ac[:, k:k + 1], 256, lambda k: MOD[:, k, 1:2])
        vT = v3(al(4 * 256), 4)
        raw = v3(al(8 * 260), 8)
        tmp = [al(256) for _ in range(4)]
        tz = V(lambda h: h.memset(raw, 0.0))
        tab = proj_small(hp, 2, 2, ab, th)
        items = []
        put, side, fin = convs(raw, 256, tmp, 4, lambda i: kT[:, i, :] if i < 4 else vT[:, i - 4, :],
                                     lambda i: 1.0 if i < 4 else None, tz)
        for blk in range(4):
            items += fm_items(hp, 256, A["win2"][2 + blk], lambda i, ps, t, blk=blk: put(2 * blk + i, ps, t), th, U)
        pipeline(items, 2, steps(side, fin, 8))
        tc = list(fin.values())
        tk = tok_from(kT, Kt, 2, tc) + tok_from(vT, Vt, 2, tc)
        t = V(lambda h: h.memset(ctxS, 0.0))
        barrier()
        top[0] = mark
        delta(2, kT, Kt, Vt, None, ab, tab, ctxS, None, [t] + tk)
        snap("ctxS", ctxS)

    def tok_from(src, dst, nt, dep):
        out = []
        for t in range(nt):
            b = banks.take()
            for i in range(4):
                p = tr(b.ap[:, i * 128:(i + 1) * 128], src[:, i, t * 128:(t + 1) * 128], *dep, *b.w, inc=(i == 3))
            e = cp(dst[:, t, :], b.ap[:, :], p, E=(S if t % 2 else None))
            b.free(e)
            out.append(e)
        return out

    def mixer2():
        reset()
        barrier()
        gate, poolT = v3(al(2048), 4), v3(al(2048), 4)
        ab = v3(al(64), 4)
        qkf2 = al(4096)
        qT, kT = v3(qkf2[:, 0:2048], 4), v3(qkf2[:, 2048:4096], 4)
        KVf = al(4096)
        Kt, Vt = v3(KVf[:, 0:2048], 4), v3(KVf[:, 2048:4096], 4)
        O = v3(al(2048), 4)
        mark = top[0]
        mTf = al(2048)
        mT = v3(mTf, 4)
        vT = v3(al(2048), 4)
        raw = v3(al(4 * 516), 4)
        ut = v3(al(2048), 4)
        tmp = [al(512) for _ in range(4)]
        U = Units(at(mark - 2048, 4096), 1024)
        hp = parts(hTf, KVf)
        th = []
        tg, tu = [], []

        def to(dst, out, half):
            def put(i, ps, t):
                out.append(cp(dst[:, i, half * 256:half * 256 + 256], ps, t, E=S))
                return out[-1]
            return put
        tz = V(lambda h: h.memset(raw, 0.0))
        put, side, fin = convs(raw, 512, tmp, 0, lambda i: (qT, kT, vT)[i // 4][:, i % 4, :],
                               lambda i: (128.0 ** -0.5, 1.0, None)[i // 4], tz)
        fm = [fm_items(hp, 512, A["win2"][blk], lambda i, ps, t, blk=blk: put(2 * blk + i, ps, t), th, U)
              for blk in range(6)]
        tm = [tok_items(hp, 4, A["win2"][6 + half], to(gate, tg, half), th, U) for half in range(2)]
        tm += [tok_items(hp, 4, A["win2"][8 + half], to(ut, tu, half), th, U) for half in range(2)]
        items = fm[0] + fm[1] + tm[0] + fm[2] + fm[3] + tm[1] + fm[4] + fm[5] + tm[2] + tm[3]
        th += norm_fm(xT, hp, lambda k: A1[:, k:k + 1], 512, lambda k: MOD[:, k, 0:1], mid=lambda: early(items, 1))
        pipeline(items, 1, steps(side, fin, 12))
        tab = proj_small(hp, 4, 2, ab, th)
        tc = list(fin.values())
        tk = tok_from(kT, Kt, 4, tc) + tok_from(vT, Vt, 4, tc)
        for g in range(4):
            s = load(A["k_box"][g])
            bx = v3(s.ap, 4)
            b = banks.take()
            for t_ in range(4):
                p = mm(b.ap[:, :], ut[:, t_, g * 128:g * 128 + 128], bx[:, t_, :], s.t, *tu, *b.w, start=(t_ == 0),
                       stop=(t_ == 3), inc=(t_ == 3))
            done(s, p)
            e = cp(mT[:, g, :], b.ap[:, :], p, E=S)
            b.free(e)
            b = banks.take()
            p = mm(b.ap[:, :], poolw[:, g * 128:(g + 1) * 128], mT[:, g, :], e, *b.w, inc=True)
            e = ts(poolT[:, g, :], b.ap[:, :], col("psc", g), ALU.mult, p)
            b.free(e)
        snap("poolT", poolT)
        barrier()
        t = V(lambda h: h.memset(O, 0.0))
        top[0] = mark
        delta(4, kT, Kt, Vt, qT, ab, tab, ctxS, O, [t] + tk)
        barrier()
        snap("O", O)
        top[0] = mark
        tmp, sq = al(2048), al(2048)
        gf = gate.rearrange("p a b -> p (a b)")
        t = silu(gf, gf, tmp)
        ms = v3(al(16), 4)
        O4 = O.rearrange("p a (g w) -> p a g w", g=4)
        t = rms_tok(O4, 4, 128, v4(sq, 4, 4), ms, row("dn").unsqueeze(1).to_broadcast([128, 4, 128]),
                    gate.rearrange("p a (g w) -> p a g w", g=4), t)
        dst = parts(hTf, qkf2)
        U = Units(KVf, 1024)
        out_w(A["wout2"], 0, lambda k: MOD[:, 16 + k, 0:1], dst,
              lambda: [fm_parts(lambda i, k=k: O[:, i, k * 128:(k + 1) * 128], dst(k), t) for k in range(4)] +
              [split(*dst(4 + k), poolT[:, k, :]) for k in range(4)], U)
        snap("x2a", xT)

    def experts():
        reset()
        barrier()
        hh, hl = al(4096), al(4096)
        grow([at(where[b4f.tensor.name], SLOT)] + [al(SLOT) for _ in range(3)])
        hp = parts(hh, hl)
        th = norm_fm(xT, hp, lambda k: A2[:, k:k + 1], 512, lambda k: MOD[:, 24 + k, 0:1], full=hT)
        snap("h2b", hT)
        ht = v3(al(4096), 4)
        th2 = []
        for i in range(4):
            for k0 in range(0, 8, 4):
                b = banks.take()
                for k in range(4):
                    p = tr(b.ap[:, k * 128:(k + 1) * 128], hT[:, k0 + k, i * 128:(i + 1) * 128], *th, *b.w, inc=(k == 3))
                e = cp(ht[:, i, k0 * 128:k0 * 128 + 512], b.ap[:, :], p, E=(S if k0 else None))
                b.free(e)
                th2.append(e)
        hd = nc.dram_tensor("h_scratch", [T, D], F32)
        t_h = misc(S, hd.ap().rearrange("(t p) d -> p t d", p=128), ht, *th2)
        lg = v3(al(64), 4)
        tl = proj_small(hp, 4, 3, lg, th)
        mx = v3(al(4), 4)
        t = V(lambda h: h.tensor_reduce(mx.squeeze(2) if False else mx[:, :, 0], lg, AX, ALU.max), tl)
        t = tt(lg, lg, mx.to_broadcast([128, 4, 16]), ALU.subtract, t)
        t = act(lg, lg, ACT.Exp, t)
        t = V(lambda h: h.tensor_reduce(mx[:, :, 0], lg, AX, ALU.add), t)
        t = rcp(mx, mx, t)
        t = tt(lg, lg, mx.to_broadcast([128, 4, 16]), ALU.mult, t)
        snap("aff", lg)
        b = banks.take()
        for i in range(4):
            p = tr(b.ap[0:16, i * 128:(i + 1) * 128], lg[:, i, :], t, *b.w, inc=(i == 3))
        wk = [al(512), al(512)]
        t = cp(wk[0][0:16, :], b.ap[0:16, :], p)
        b.free(t)
        vals = al(64)
        idx = memu[:, 0:64]
        for r in range(8):
            v8 = vals[0:16, 8 * r:8 * r + 8]
            a, bb = wk[r % 2][0:16, :], wk[(r + 1) % 2][0:16, :]
            t = V(lambda h, v8=v8, a=a: h.max(v8, a), t)
            t1 = V(lambda h, v8=v8, a=a, r=r: h.max_index(idx[0:16, 8 * r:8 * r + 8], v8, a), t)
            t = V(lambda h, v8=v8, a=a, bb=bb: h.match_replace(bb, v8, a, -1.0), t1)
        idd = nc.dram_tensor("idx_scratch", [1024], U32)
        vd = nc.dram_tensor("val_scratch", [1024], F32)
        t1 = misc(S, idd.ap().rearrange("(e c) -> e c", e=16), idx[0:16, :], t)
        t2 = misc(S, vd.ap().rearrange("(e c) -> e c", e=16), vals[0:16, :], t)
        ixT, vT = memu[:, 64:72], al(8)
        t1 = misc(S, ixT, idd.ap().rearrange("(j p) -> p j", p=128), t1, slow=True)
        t2 = misc(S, vT, vd.ap().rearrange("(j p) -> p j", p=128), t2, slow=True)
        ixf = al(8)
        tix = cp(ixf, ixT, t1)
        V.wait(t2)
        S.wait(t2)
        snap("ixf", ixf)
        iot = al(512)
        ti = G(lambda h: h.iota(iot, [[1, 512]], base=0, channel_multiplier=0, allow_small_or_imprecise_dtypes=True))
        piece = lambda i: (hh, hl)[i // 4][:, (i % 4) * 1024:(i % 4) * 1024 + 1024]
        xe = [piece(0), piece(1)]
        xeT = [v3(piece(2), 8), v3(piece(3), 8)]
        hid = [piece(4), piece(5)]
        hidT = [v3(piece(6), 8), v3(piece(7), 8)]
        ye = [al(1024) for _ in range(2)]
        oh = [al(512) for _ in range(2)]
        ex = [al(512) for _ in range(2)]
        exr = [None, None]
        xe_r, xeT_r, hid_r, hidT_r, ye_r = ([None, None] for _ in range(5))
        gs = [nc.alloc_semaphore(f"gather{i}") for i in range(8)]
        for pr in range(8):
            x = pr % 2
            G.wait(t_h, t1, xe_r[x])
            G.q.append(lambda pr=pr, x=x: nc.gpsimd.indirect_dma_start(
                xe[x], None, hd.ap(), bass.IndirectOffsetOnAxis(ap=ixT[:, pr:pr + 1], axis=0)).then_inc(gs[pr], 16))
            tgat = (gs[pr], 16)
            toh = ts(oh[x], iot, ixf[:, pr:pr + 1], ALU.is_equal, ti, tix, ye_r[x])
            tx = []
            for k0 in range(0, 8, 4):
                b = banks.take()
                for k in range(4):
                    p = tr(b.ap[:, k * 128:(k + 1) * 128], xe[x][:, (k0 + k) * 128:(k0 + k + 1) * 128], tgat, *b.w,
                           inc=(k == 3))
                e = cp(xeT[x][:, k0:k0 + 4, :], v3(b.ap[:, :], 4), p, xeT_r[x], E=(S if k0 else None))
                b.free(e)
                tx.append(e)
            xe_r[x] = p

            def wide(w, lhs, dep, half):
                b = banks.take()
                for e_ in range(2):
                    for kh in range(2):
                        s = load(A[w][(2 * pr + e_) * 4 + half * 2 + kh])
                        w4 = v3(s.ap, 4)
                        for k in range(4):
                            kk = kh * 4 + k
                            p = mm(b.ap[64 * e_:64 * e_ + 64, :], lhs[:, kk, 64 * e_:64 * e_ + 64], w4[:, k, :], s.t,
                                   *dep, *b.w, start=(kk == 0), stop=(kk == 7), inc=(k == 3))
                        done(s, p)
                return b, p
            th_ = []
            for half in range(2):
                bg, pg = wide("eg", xeT[x], tx, half)
                bu, pu = wide("eu", xeT[x], tx, half)
                e = ex[half]
                t = act(e, bg.ap[:, :], ACT.Tanh, pg, exr[half], scale=0.5)
                t = stt(e, e, 1.0, bg.ap[:, :], ALU.add, ALU.mult, t)
                bg.free(t)
                t = tt(hid[x][:, half * 512:half * 512 + 512], e, bu.ap[:, :], ALU.mult, t, pu, hid_r[x])
                bu.free(t)
                exr[half] = t
                th_.append(t)
            xeT_r[x] = pu
            tx = []
            for k0 in range(0, 8, 4):
                b = banks.take()
                for k in range(4):
                    p = tr(b.ap[:, k * 128:(k + 1) * 128], hid[x][:, (k0 + k) * 128:(k0 + k + 1) * 128], *th_, *b.w,
                           inc=(k == 3))
                e = cp(hidT[x][:, k0:k0 + 4, :], v3(b.ap[:, :], 4), p, hidT_r[x], E=(S if k0 else None))
                b.free(e)
                tx.append(e)
            hid_r[x] = p
            ty = []
            for half in range(2):
                bd, pd = wide("ed", hidT[x], tx, half)
                t = ts(ye[x][:, half * 512:half * 512 + 512], bd.ap[:, :], vT[:, pr:pr + 1], ALU.mult, pd, ye_r[x],
                       s2=0.5, op1=ALU.mult)
                bd.free(t)
                ty.append(t)
            hidT_r[x] = pd
            for k in range(8):
                b = banks.take()
                p = mm(b.ap[:, :], ye[x][:, k * 128:(k + 1) * 128], oh[x], *ty, toh, *b.w, inc=True)
                t = stt(xT[:, k, :], b.ap[:, :], MOD[:, 40 + k, 0:1], xT[:, k, :], ALU.mult, ALU.add, p)
                b.free(t)
                if pr == 7:
                    stat_add(k, xT[:, k, :], t)
            ye_r[x] = p

    def output():
        reset()
        barrier()
        hh, hl = al(4096), al(4096)
        t = norm_fm(xT, parts(hh, hl), lambda k: col("normf", k), 512, full=hT)
        ot = [al(1024) for _ in range(4)]
        for i in range(4):
            es = []
            for k0 in range(0, 8, 4):
                b = banks.take()
                for k in range(4):
                    p = tr(b.ap[:, k * 128:(k + 1) * 128], hT[:, k0 + k, i * 128:(i + 1) * 128], *t, *b.w, inc=(k == 3))
                e = cp(ot[i][:, k0 * 128:k0 * 128 + 512], b.ap[:, :], p, E=(S if k0 else None))
                b.free(e)
                es.append(e)
            misc(S, out_x[i * 128:(i + 1) * 128, :], ot[i], *es)

    def start():
        reset()
        barrier()
        tb = rel_table()
        for e in (V, PE):
            e.wait(tb)
        reset()
        barrier()
        xt0 = v3(al(4096), 4)
        t = misc(S, xt0, A["x"].rearrange("(t p) d -> p t d", p=128))
        to_fm(xt0, xT, 4, t, stats=True)

    stages = [modulation, context, start]
    for l in range(2):
        stages += [lambda l=l: ffn(2 * l, f"n1_{l}"), lambda l=l: snap(f"xa{l}", xT), lambda l=l: mixer(l),
                   lambda l=l: snap(f"xb{l}", xT), lambda l=l: ffn(2 * l + 1, f"n2_{l}"),
                   lambda l=l: snap(f"xc{l}", xT)]
    stages += [mixer2, experts, output]
    if isinstance(upto, int):
        stages = stages[:upto]
    else:
        stages = [s for i, s in enumerate(stages) if i in upto]
    for s in stages:
        s()
    SP.wait(*dma_all)
    SP.wait(*every())

    with nc.Block() as block:
        @block.sync
        def _(e):
            SP.run()

        @block.scalar
        def _(e):
            S.run()

        @block.vector
        def _(e):
            V.run()

        @block.gpsimd
        def _(e):
            G.run()

        @block.tensor
        def _(e):
            PE.run()
    return {e.name: len(e.q) for e in (PE, V, S, G, SP)}


def lay_out(i):
    f = lambda a: np.asarray(a)
    o = {}

    def blocks(w, nk, nc_):
        K_, N = w.shape
        a = w.reshape(K_ // (128 * nk), nk, 128, N // nc_, nc_).transpose(3, 0, 2, 1, 4)
        return a.reshape(-1, 128, nk * nc_)

    pairs = [("ffn1", 0), ("ffn2", 0), ("ffn1", 1), ("ffn2", 1)]
    o["wg"] = np.stack([blocks(f(i[n + "_w_gate"])[l], 8, 256) for n, l in pairs])
    o["wu"] = np.stack([blocks(f(i[n + "_w_up"])[l], 8, 256) for n, l in pairs])
    o["wd0"] = np.stack([blocks(f(i[n + "_w_down"])[l, 0:1536], 12, 128) for n, l in pairs])
    o["wd1"] = np.stack([blocks(f(i[n + "_w_down"])[l, 1536:], 10, 128) for n, l in pairs])
    w = f(i["w_in"])
    fm = np.concatenate([w[:, :, 0:512], w[:, :, 1544:2568], w[:, :, 2576:3088], w[:, :, 512:1024],
                         w[:, :, 1032:1544], w[:, :, 3088:3344]], 2)
    o["win"] = np.stack([blocks(fm[l], 8, 256) for l in range(2)])
    o["wout"] = np.stack([blocks(f(i["w_out"])[l], 8, 256) for l in range(2)])
    w2 = f(i["w_in_2"])[0]
    o["win2"] = blocks(np.concatenate([w2[:, 0:1536], w2[:, 1552:2576]], 1), 8, 256)
    o["wout2"] = blocks(f(i["w_out_2"])[0], 8, 256)[None]
    o["wmod"] = blocks(f(i["w_mod_2"])[0], 4, 512)
    for n, k in (("eg", "w_gate_2"), ("eu", "w_up_2"), ("ed", "w_down_2")):
        w = f(i[k])[0]
        o[n] = w.reshape(16, 2, 4, 128, 2, 512).transpose(0, 4, 1, 3, 2, 5).reshape(64, 128, 2048)
    k8 = lambda a: a.reshape(8, 128, -1).transpose(1, 0, 2).reshape(128, -1)
    sm = [np.concatenate([w_[:, 1024:1032], w_[:, 2568:2576]], 1) for w_ in f(i["w_in"])]
    o["smallw"] = np.concatenate([k8(sm[0]), k8(sm[1]), k8(w2[:, 1536:1552]), k8(f(i["w_router_2"])[0])], 1)
    o["poolw"] = f(i["pool_w_2"])[0].transpose(1, 0, 2).reshape(128, 512)
    c8 = lambda a: a.reshape(-1, 128).T
    cols, rows = {}, {}
    for l in range(2):
        cols[f"n1_{l}"] = c8(f(i["ffn1_norm_w"])[l])
        cols[f"nm_{l}"] = c8(f(i["mix_norm_w"])[l])
        cols[f"n2_{l}"] = c8(f(i["ffn2_norm_w"])[l])
        cols[f"cw_{l}"] = f(i["ssm_conv_w"])[l].reshape(4, 8, 128).transpose(2, 1, 0).reshape(128, 32)
        cols[f"cb_{l}"] = c8(f(i["ssm_conv_b"])[l])
        cols[f"qw_{l}"] = np.tile(f(i["diff_q_norm_w"])[l].reshape(64), 2)[:, None]
        cols[f"kw_{l}"] = np.tile(f(i["diff_k_norm_w"])[l].reshape(64), 2)[:, None]
        gb = np.concatenate([f(i["mlstm_gate_bias"])[l].reshape(8), f(i["ssm_dt_bias"])[l]])
        rows[f"gb_{l}"] = np.tile(gb, 4)
        rows[f"al_{l}"] = np.tile(f(i["ssm_A_log"])[l], 4)
        rows[f"mn_{l}"] = f(i["mlstm_norm_w"])[l]
        rows[f"sn_{l}"] = f(i["ssm_norm_w"])[l]
        rows[f"D_{l}"] = f(i["ssm_D"])[l]
        rows[f"sl_{l}"] = f(i["diff_subln_w"])[l]
        rows[f"lam_{l}"] = f(i["diff_lambda"])[l].reshape(128)
    cols["norm1"] = c8(f(i["norm1_2"])[0])
    cols["norm2"] = c8(f(i["norm2_2"])[0])
    cols["normf"] = c8(f(i["norm_f_2"]))
    cols["cw2"] = f(i["conv_w_2"])[0].reshape(4, 12, 128).transpose(2, 1, 0).reshape(128, 48)
    cols["psc"] = c8(f(i["pool_scale_2"])[0])
    cols["c"] = np.stack([c8(f(i["c_2"])[0]), c8(f(i["c_ctx_2"]))], 2).reshape(128, 16)
    cols["bmod"] = c8(f(i["b_mod_2"])[0])
    rows["al2"] = f(i["a_log_2"])[0].reshape(8)
    rows["dtb2"] = f(i["dt_bias_2"])[0].reshape(8)
    rows["dn"] = f(i["dn_norm_2"])[0]
    o["cols"] = np.concatenate([cols[n] for n, _ in COLS], 1)
    o["rows"] = np.tile(np.concatenate([rows[n] for n, _ in ROWS])[None], (128, 1))
    o["rel_bias"] = f(i["rel_bias"])
    o["x"] = f(i["x"])[0]
    o["ctx"] = f(i["ctx_2"])[0]
    o["k_const"], o["k_sel"], o["k_oh"], o["k_neg"], o["k_box"] = const_arrays()
    return {n: np.ascontiguousarray(a) for n, a in o.items()}


def kernel(**inputs):
    import concourse.bacc as _bacc
    from concourse.bass_utils import run_bass_kernel_spmd as _run

    nc = _bacc.Bacc("TRN2", target_bir_lowering=False, num_devices=1)
    arrays = {"in_" + n: a for n, a in lay_out(inputs).items()}
    A = {n[3:]: nc.dram_tensor(n, a.shape, mybir.dt.from_np(a.dtype), kind="ExternalInput").ap()
         for n, a in arrays.items()}
    out = nc.dram_tensor("out_x", (T, D), F32, kind="ExternalOutput").ap()
    build(nc, A, out)
    r = _run(nc, [arrays], core_ids=[0])
    return r.results[0]["out_x"].reshape(1, T, D)
```
